# Optimizing a Trainium2 kernel written in Bass

```python
import jax, jax.numpy as jnp
from jax import lax
import numpy as np

D_MODEL = 1024
BATCH = 1
SEQ = 1024
DEPTH = 1

ML_WIDTH = D_MODEL // 2
ML_HEADS = 4
ML_HEAD_DIM = ML_WIDTH // ML_HEADS
ML_CHUNK = 128
G_WIDTH = D_MODEL // 4
G_HEADS = 4
G_HEAD_DIM = G_WIDTH // G_HEADS
G_CHUNK = 128
C_WIDTH = D_MODEL // 4
C_GROUPS = 4
CONV_WIDTH = 31
MIX_WIDTH = ML_WIDTH + G_WIDTH + C_WIDTH
P_IN = 4 * ML_WIDTH + 2 * ML_HEADS + 2 * G_WIDTH + 2 * C_WIDTH
N_EXPERTS = 16
N_GROUPS = 4
EXPERTS_PER_GROUP = N_EXPERTS // N_GROUPS
TOP_K = 2
D_EXPERT = D_MODEL // 2
DEEPNORM_ALPHA = (2.0 * DEPTH) ** 0.25
DEEPNORM_BETA = (8.0 * DEPTH) ** -0.25
LN_EPS = 1e-5

kernel_name = "hybrid_mlstm_gmlp_conv_groupmoe_deepnorm"

def layer_norm(x, w, b, eps=LN_EPS):
    xf = x.astype(jnp.float32)
    mu = xf.mean(-1, keepdims=True)
    var = jnp.square(xf - mu).mean(-1, keepdims=True)
    return ((xf - mu) * lax.rsqrt(var + eps) * w.astype(jnp.float32) + b.astype(jnp.float32)).astype(x.dtype)

def mlstm_chunkwise(q, k, v, i_pre, f_pre):
    B_, S_, H_, Dh = q.shape
    L = ML_CHUNK
    NC = S_ // L
    f32 = jnp.float32

    def chunks(t):
        return t.astype(f32).reshape(B_, NC, L, H_, -1).transpose(0, 3, 1, 2, 4)

    q_c = chunks(q)
    k_c = chunks(k) * (Dh ** -0.5)
    v_c = chunks(v)
    logi = i_pre.astype(f32).reshape(B_, NC, L, H_).transpose(0, 3, 1, 2)
    logf = jax.nn.log_sigmoid(f_pre.astype(f32)).reshape(B_, NC, L, H_).transpose(0, 3, 1, 2)
    b = jnp.cumsum(logf, axis=-1)
    g = b[..., -1]
    a = g[..., None] - b + logi

    def step(carry, xs):
        C, n, m = carry
        k_j, v_j, a_j, g_j = xs
        m_new = jnp.maximum(g_j + m, a_j.max(-1))
        w = jnp.exp(a_j - m_new[..., None])
        decay = jnp.exp(g_j + m - m_new)
        C_new = decay[..., None, None] * C + jnp.einsum('bhl,bhld,bhle->bhde', w, k_j, v_j)
        n_new = decay[..., None] * n + jnp.einsum('bhl,bhld->bhd', w, k_j)
        return (C_new, n_new, m_new), (C, n, m)

    init = (jnp.zeros((B_, H_, Dh, Dh), f32), jnp.zeros((B_, H_, Dh), f32), jnp.zeros((B_, H_), f32))
    xs = (jnp.moveaxis(k_c, 2, 0), jnp.moveaxis(v_c, 2, 0), jnp.moveaxis(a, 2, 0), jnp.moveaxis(g, 2, 0))
    _, (C_prev, n_prev, m_prev) = lax.scan(step, init, xs)
    C_prev = jnp.moveaxis(C_prev, 0, 2)
    n_prev = jnp.moveaxis(n_prev, 0, 2)
    m_prev = jnp.moveaxis(m_prev, 0, 2)

    causal = jnp.tril(jnp.ones((L, L), bool))
    log_d = jnp.where(causal, b[..., :, None] - b[..., None, :] + logi[..., None, :], -jnp.inf)
    log_inter = b + m_prev[..., None]
    m_row = jnp.maximum(log_inter, log_d.max(-1))
    p = jnp.einsum('bhcld,bhcsd->bhcls', q_c, k_c) * jnp.exp(log_d - m_row[..., None])
    w_inter = jnp.exp(log_inter - m_row)
    num = jnp.einsum('bhcls,bhcsd->bhcld', p, v_c) + w_inter[..., None] * jnp.einsum('bhcld,bhcde->bhcle', q_c, C_prev)
    den = p.sum(-1) + w_inter * jnp.einsum('bhcld,bhcd->bhcl', q_c, n_prev)
    h = num / jnp.maximum(jnp.abs(den), jnp.exp(-m_row))[..., None]
    return h.transpose(0, 2, 3, 1, 4).reshape(B_, S_, H_ * Dh)

def mixer(x, w_in, b_in, mlstm_norm_w, gmlp_norm_w, gmlp_norm_b, gmlp_ws, gmlp_bs,
          conv_w, conv_b, conv_norm_w, conv_norm_b, w_out):
    B_, S_, _ = x.shape
    proj = x @ w_in + b_in
    sizes = (ML_WIDTH,) * 4 + (ML_HEADS,) * 2 + (G_WIDTH,) * 2 + (C_WIDTH,) * 2
    q, k, v, o, i_pre, f_pre, gu, gv, ca, cb = jnp.split(proj, np.cumsum(sizes)[:-1].tolist(), axis=-1)

    heads = lambda t: t.reshape(B_, S_, ML_HEADS, ML_HEAD_DIM)
    h = mlstm_chunkwise(heads(q), heads(k), heads(v), i_pre, f_pre)
    hh = h.reshape(B_, S_, ML_HEADS, ML_HEAD_DIM)
    mu = hh.mean(-1, keepdims=True)
    var = jnp.square(hh - mu).mean(-1, keepdims=True)
    hh = ((hh - mu) * lax.rsqrt(var + 1e-6)).reshape(B_, S_, ML_WIDTH) * mlstm_norm_w.astype(jnp.float32)
    h_a = (jax.nn.sigmoid(o.astype(jnp.float32)) * hh).astype(x.dtype)

    u = jax.nn.gelu(gu)
    z = layer_norm(jax.nn.gelu(gv), gmlp_norm_w, gmlp_norm_b)
    z = z.reshape(B_, S_ // G_CHUNK, G_CHUNK, G_HEADS, G_HEAD_DIM)
    ws = gmlp_ws * jnp.tril(jnp.ones((G_CHUNK, G_CHUNK), gmlp_ws.dtype))
    z = jnp.einsum('hts,bcshd->bcthd', ws, z) + gmlp_bs.T[:, :, None]
    h_b = u * z.reshape(B_, S_, G_WIDTH)

    c = ca * jax.nn.sigmoid(cb)
    c = lax.conv_general_dilated(c, conv_w[:, None, :], window_strides=(1,),
                                 padding=[(CONV_WIDTH - 1, 0)],
                                 dimension_numbers=('NWC', 'WIO', 'NWC'),
                                 feature_group_count=C_WIDTH) + conv_b
    h_c = jax.nn.silu(layer_norm(c, conv_norm_w, conv_norm_b))

    return jnp.concatenate([h_a, h_b, h_c], axis=-1) @ w_out

def moe(x, router_w, router_b, w_gate, w_up, w_down):
    B_, S_, D_ = x.shape
    xt = x.reshape(B_ * S_, D_)
    s = jax.nn.sigmoid(xt.astype(jnp.float32) @ router_w.astype(jnp.float32))
    sel = s + router_b.astype(jnp.float32)
    gscore = lax.top_k(sel.reshape(-1, N_GROUPS, EXPERTS_PER_GROUP), 2)[0].sum(-1)
    gidx = jnp.argmax(gscore, axis=-1)
    in_group = (jnp.arange(N_EXPERTS) // EXPERTS_PER_GROUP)[None, :] == gidx[:, None]
    _, eidx = lax.top_k(jnp.where(in_group, sel, -jnp.inf), TOP_K)
    gate = jnp.take_along_axis(s, eidx, axis=1)
    gate = gate / gate.sum(-1, keepdims=True)
    combine = (jax.nn.one_hot(eidx, N_EXPERTS, dtype=jnp.float32) * gate[..., None]).sum(1).astype(x.dtype)
    out = jnp.zeros_like(xt)
    for e in range(N_EXPERTS):
        hid = jax.nn.silu(xt @ w_gate[e]) * (xt @ w_up[e])
        out = out + combine[:, e:e + 1] * (hid @ w_down[e])
    return out.reshape(B_, S_, D_)

def setup_inputs(seed: int = 0) -> dict:
    key = jax.random.key(seed)
    ks = jax.random.split(key, 24)
    f32 = jnp.float32
    nrm = lambda k, shape, scale: jax.random.normal(k, shape, f32) * scale
    L = DEPTH
    x = nrm(ks[0], (BATCH, SEQ, D_MODEL), 1.0)
    v_lo = 2 * ML_WIDTH
    w_in = nrm(ks[1], (L, D_MODEL, P_IN), D_MODEL ** -0.5)
    w_in = w_in.at[:, :, v_lo:v_lo + ML_WIDTH].multiply(DEEPNORM_BETA)
    f_lo = 4 * ML_WIDTH + ML_HEADS
    b_in = nrm(ks[2], (L, P_IN), 0.02).at[:, f_lo:f_lo + ML_HEADS].add(jnp.linspace(3.0, 6.0, ML_HEADS))
    mlstm_norm_w = 1.0 + nrm(ks[3], (L, ML_WIDTH), 0.02)
    gmlp_norm_w = 1.0 + nrm(ks[4], (L, G_WIDTH), 0.02)
    gmlp_norm_b = nrm(ks[5], (L, G_WIDTH), 0.02)
    gmlp_ws = nrm(ks[6], (L, G_HEADS, G_CHUNK, G_CHUNK), G_CHUNK ** -0.5)
    gmlp_bs = 1.0 + nrm(ks[7], (L, G_HEADS, G_CHUNK), 0.02)
    conv_w = nrm(ks[8], (L, CONV_WIDTH, C_WIDTH), CONV_WIDTH ** -0.5)
    conv_b = nrm(ks[9], (L, C_WIDTH), 0.02)
    conv_norm_w = 1.0 + nrm(ks[10], (L, C_WIDTH), 0.02)
    conv_norm_b = nrm(ks[11], (L, C_WIDTH), 0.02)
    w_out = nrm(ks[12], (L, MIX_WIDTH, D_MODEL), MIX_WIDTH ** -0.5 * DEEPNORM_BETA)
    ln1_w = 1.0 + nrm(ks[13], (L, D_MODEL), 0.02)
    ln1_b = nrm(ks[14], (L, D_MODEL), 0.02)
    router_w = nrm(ks[15], (D_MODEL, N_EXPERTS), D_MODEL ** -0.5)
    router_b = nrm(ks[16], (N_EXPERTS,), 0.01)
    w_gate = nrm(ks[17], (L, N_EXPERTS, D_MODEL, D_EXPERT), D_MODEL ** -0.5)
    w_up = nrm(ks[18], (L, N_EXPERTS, D_MODEL, D_EXPERT), D_MODEL ** -0.5)
    w_down = nrm(ks[19], (L, N_EXPERTS, D_EXPERT, D_MODEL), D_EXPERT ** -0.5 * DEEPNORM_BETA)
    ln2_w = 1.0 + nrm(ks[20], (L, D_MODEL), 0.02)
    ln2_b = nrm(ks[21], (L, D_MODEL), 0.02)
    return {"x": x, "w_in": w_in, "b_in": b_in, "mlstm_norm_w": mlstm_norm_w,
            "gmlp_norm_w": gmlp_norm_w, "gmlp_norm_b": gmlp_norm_b, "gmlp_ws": gmlp_ws, "gmlp_bs": gmlp_bs,
            "conv_w": conv_w, "conv_b": conv_b, "conv_norm_w": conv_norm_w, "conv_norm_b": conv_norm_b,
            "w_out": w_out, "ln1_w": ln1_w, "ln1_b": ln1_b, "router_w": router_w, "router_b": router_b,
            "w_gate": w_gate, "w_up": w_up, "w_down": w_down, "ln2_w": ln2_w, "ln2_b": ln2_b}

def reference(x, w_in, b_in, mlstm_norm_w, gmlp_norm_w, gmlp_norm_b, gmlp_ws, gmlp_bs,
              conv_w, conv_b, conv_norm_w, conv_norm_b, w_out, ln1_w, ln1_b, router_w, router_b,
              w_gate, w_up, w_down, ln2_w, ln2_b):
    for l in range(DEPTH):
        y = mixer(x, w_in[l], b_in[l], mlstm_norm_w[l], gmlp_norm_w[l], gmlp_norm_b[l], gmlp_ws[l], gmlp_bs[l],
                  conv_w[l], conv_b[l], conv_norm_w[l], conv_norm_b[l], w_out[l])
        x = layer_norm(DEEPNORM_ALPHA * x + y, ln1_w[l], ln1_b[l])
        y = moe(x, router_w, router_b, w_gate[l], w_up[l], w_down[l])
        x = layer_norm(DEEPNORM_ALPHA * x + y, ln2_w[l], ln2_b[l])
    return x


_drawn_inputs = setup_inputs


def setup_inputs(seed=0):
    import zlib

    import numpy as np

    out = dict(_drawn_inputs(seed))
    spreads = {}
    factors = {'mlstm_norm_w': 4.084,
     'gmlp_norm_w': 8.0,
     'gmlp_norm_b': 5.277,
     'gmlp_bs': 8.0,
     'conv_b': 2.928,
     'conv_norm_w': 4.363,
     'conv_norm_b': 4.345,
     'ln2_w': 2.952,
     'ln2_b': 2.749}
    for name, (base, spread) in spreads.items():
        noise = np.random.default_rng([zlib.crc32(name.encode()), seed]).standard_normal(out[name].shape)
        drawn = base * np.exp(spread * noise) if base else spread * noise
        out[name] = __import__('jax').numpy.asarray(drawn.astype(out[name].dtype))
    for name, factor in factors.items():
        out[name] = (out[name] * factor).astype(out[name].dtype)
    return out
```

```python
from contextlib import ExitStack

import concourse.bass as bass
import numpy as np
from concourse import mybir

F32 = mybir.dt.float32
F32R = mybir.dt.float32r
I32 = mybir.dt.int32
ALU = mybir.AluOpType
AF = mybir.ActivationFunctionType
AX = mybir.AxisListType

P = 128
D = 1024
SEQ = 1024
KC = D // P
T = SEQ // P
HEADS = 4
DH = 128
MLW = HEADS * DH
GW = 256
GHD = GW // HEADS
CW = 256
TAPS = 31
NE = 16
NG = 4
EG = NE // NG
DE = 512
FC = DE // P
ALPHA = 2.0 ** 0.25
LN_EPS = 1e-5
ML_EPS = 1e-6
KSCALE = DH ** -0.5
GELU_IN = HEADS * 2
NEG = -1.0e30
TILES_MAX = (2 * SEQ + NE * (P - 1)) // P
SMALL = 1120
UNITS = 12

C_Q, C_K, C_V, C_O, C_GATE = 0, MLW, 2 * MLW, 3 * MLW, 4 * MLW
C_GU = C_GATE + 2 * HEADS
C_GV = C_GU + GW
C_CA = C_GV + GW
C_CB = C_CA + CW
GROUPS = [(C_GATE, 2 * HEADS + GW), (C_GV, GW), (C_CA, 2 * CW), (C_Q, MLW), (C_K, MLW), (C_V, MLW), (C_O, MLW)]
JOBS = 8

PRIMED = 1


class Links:

    def __init__(self, eng, sem, name):
        self.eng, self.sem, self.n = eng, sem, 0
        self.reg = eng.alloc_register(name)
        eng.reg_mov(self.reg, 0)
        self.base = 0

    def done(self, ins):
        self.n += 1
        ins.then_inc(self.sem, 1)
        return self.base + self.n

    def link(self, ins):
        self.eng.wait_ge(self.sem, self.done(ins))

    def settle(self):
        if self.n:
            self.eng.reg_add(self.reg, self.reg, self.n)
        self.n = 0
        self.base = self.eng.snap(self.reg)


def hybrid_kernel(nc, x, w_in, b_in, mlstm_norm_w, gmlp_norm_w, gmlp_norm_b, gmlp_ws, gmlp_bs,
                  conv_w, conv_b, conv_norm_w, conv_norm_b, w_out, ln1_w, ln1_b, router_w, router_b,
                  w_gate, w_up, w_down, ln2_w, ln2_b, out):
    ctx = ExitStack()
    with ctx:
        def sb(name, shape, dt=F32):
            return ctx.enter_context(nc.sbuf_tensor(name, shape, dt))

        def sem(name):
            return ctx.enter_context(nc.semaphore(name))

        def dram(name, shape, dt=F32):
            return nc.dram_tensor(name, shape, dt, kind="Internal").ap()

        x_tiles = x[0].rearrange("(t p) n -> t p n", p=P)
        out_tiles = out[0].rearrange("(t p) n -> t p n", p=P)
        win_v = w_in[0].rearrange("(p k) n -> p k n", k=KC)
        wout_v = w_out[0].rearrange("(k p) n -> k p n", p=P)
        gate_v = w_gate[0].rearrange("e (p k) n -> e p k n", k=KC)
        up_v = w_up[0].rearrange("e (p k) n -> e p k n", k=KC)
        down_v = w_down[0].rearrange("e (p f) n -> e p f n", f=FC)

        k_dram = dram("k_scratch", (SEQ, MLW))
        v_dram = dram("v_scratch", (SEQ, MLW))
        og_dram = dram("og_scratch", (SEQ, MLW))
        hb_dram = dram("hb_scratch", (SEQ, GW))
        q_dram = dram("q_scratch", (P, HEADS, SEQ))
        nm_dram = dram("nm_scratch", (T * HEADS, P))
        x1_dram = dram("x1_scratch", (SEQ, D))
        y_dram = dram("y_scratch", ((TILES_MAX + 1) * P, D))

        WR = sb("split_weights", [P, 24576], F32R)
        XR = sb("split_rows", [P, 2, KC, P], F32R)
        HR = sb("split_hidden", [P, 2, FC, P], F32R)
        xT = WR[:, 0:16384].rearrange("p (h k n) -> p h k n", h=2, k=KC)
        wc = WR[:, 16384:24576].rearrange("p (h k n) -> p h k n", h=2, k=KC)
        wo = xT
        wg = wc
        wu = WR[:, 0:8192].rearrange("p (h k n) -> p h k n", h=2, k=KC)
        wd = WR[:, 8192:16384].rearrange("p (h k n) -> p h k n", h=2, k=FC)

        arena = sb("arena", [P, 12352 + 2048])
        stage = arena[:, 0:12288].rearrange("p (s n) -> p s n", s=UNITS)
        cpad = arena[:, 8192:8192 + 2 * 1056].rearrange("p (f n) -> p f n", f=2)
        gvs = arena[:, 10304:10304 + 2048].rearrange("p (t n) -> p t n", t=T)
        acc = arena[:, 12352:14400].rearrange("p (f n) -> p f n", f=2)
        rows = arena[:, 8192:12288].rearrange("p (s n) -> p s n", s=4)
        NF = 9130
        work = sb("work", [P, NF])
        used = {"a": 0, "b": 0, "c": 0, "d": 0}

        def at(phase, *shape):
            n = int(np.prod(shape))
            o = used[phase]
            used[phase] = o + n
            assert used[phase] <= NF, (phase, used[phase])
            v = work[:, o:o + n]
            if len(shape) == 2:
                v = v.rearrange("p (a b) -> p a b", a=shape[0])
            elif len(shape) == 3:
                v = v.rearrange("p (a b c) -> p a b c", a=shape[0], b=shape[1])
            return v

        ident = sb("ident", [P, P])
        tri = sb("tri", [P, P])
        ones = sb("ones", [P, P])
        small = sb("small", [P, SMALL])
        small_used = [0]

        def sm(*shape):
            n = int(np.prod(shape))
            o = small_used[0]
            small_used[0] = o + n
            assert o + n <= SMALL, o + n
            v = small[:, o:o + n]
            if len(shape) == 2:
                v = v.rearrange("p (a b) -> p a b", a=shape[0])
            elif len(shape) == 3:
                v = v.rearrange("p (a b c) -> p a b c", a=shape[0], b=shape[1])
            return v

        NC_ = T * HEADS
        uS = sm(NC_)
        w4 = sm(4, NC_)
        logits = sm(T, NE)
        cols = sm(80)
        convw = cols[:, 0:2 * TAPS].rearrange("p (f j) -> p f j", f=2)
        convc = cols[:, 2 * TAPS:2 * TAPS + 6].rearrange("p (i f) -> p i f", i=3)
        bs_col = cols[:, 68:72]
        bq_fm = cols[:, 72:80]
        slot = sm(2, T)
        gatew = sm(2, T)
        st_a = sm(T, 6)
        mv_a = sm(T, 2)
        rs_a = sm(T)
        st_b = sm(HEADS, 6)
        mv_b = sm(HEADS, 2)
        rs_b = sm(HEADS)
        den = sm(HEADS)
        st_c = sm(2, 6)
        mv_c = sm(2)
        rs_c = sm(1)
        mv_f = sm(T, 2)
        rs_f = sm(T)
        rb = sm(NE)
        i_lo = sm(P)
        i_desc = sm(NE)
        i_thr = sm(T - 1)
        i_tok = sm(T)
        tok1 = sb("tile_tokens", [P, 1], I32)[:, :]
        parts = sb("slot_parts", [P, 2, 2, T], I32)
        sloti = sb("slot_index", [P, 2, T], I32)
        tok = sb("token_index", [P, 32], I32)
        ntiles = sb("extra_tiles", [1, NE + 1], I32)



        b_tm = at("a", 5, 512)
        mlw = at("a", MLW)
        gnw = at("a", 2, GW)
        ev = at("a", 4, 512)
        ug = at("a", T, GW)
        gates = at("a", T, 2 * HEADS)
        wsT = at("a", HEADS, P)
        wsl = ev[:, 2, :].rearrange("p (h n) -> p h n", h=HEADS)
        packed = ev[0:80, 3, 0:P]
        gt = at("a", 10, NC_)
        gT = at("a", 3, P)
        grow = at("a", 5, NC_)
        kin = at("b", HEADS, DH)
        qin = at("b", HEADS, P)
        vau = at("b", HEADS, DH + 1)
        kTv = at("b", HEADS * (DH + 1))
        kT = kTv[:, 0:HEADS * P].rearrange("p (h n) -> p h n", h=HEADS)
        vw = kTv.rearrange("p (h n) -> p h n", h=HEADS)
        nm = at("b", HEADS, P)
        num = at("b", HEADS, DH + 1)
        og = at("b", MLW)
        hbin = at("b", GW)
        C = at("b", HEADS, DH + 1)
        ha = at("b", HEADS, DH)
        nmask = at("b", P)
        ln1 = at("b", 2, D)
        rw = at("b", KC, NE)
        xin, x1s, x1T, sq = (rows[:, i] for i in range(4))
        rt = work[:, 0:5 * T * NE].rearrange("p (i t e) -> p i t e", i=5, t=T)
        used["c"] = 5 * T * NE
        disp = at("c", T, NE)
        pairs = at("c", T * NG, 6)
        gsc = at("c", T, NG)
        gsel = at("c", T, NG)
        mx = at("c", T)
        cnt = at("c", 5, NE)
        more_than = at("c", NE, T - 1)
        hot_lo = at("c", 2 * T, P)
        hot_hi = at("c", 2 * T, 32)
        partf = at("c", 2, 2, T)
        stri = at("c", P)
        xe = at("d", D)
        sil = at("d", DE)
        hid = at("d", DE)
        ys = at("d", D)
        ln2 = at("d", 2, D)
        psum = ctx.enter_context(nc.psum_tensor("banks", [P, 8, 512], F32))

        def bank(i):
            return psum[:, i, :]

        def by_rows(v):
            return v.partition_broadcast(P)

        small_loads = [(b_tm[:, i, 0:w], by_rows(b_in[0, c:c + w])) for i, (c, w) in
                       enumerate(((C_GATE, 2 * HEADS + GW), (C_GV, GW), (C_K, MLW), (C_V, MLW), (C_O, MLW)))]
        small_loads += [(wsl, gmlp_ws[0].rearrange("h t s -> t h s")),
                        (mlw, by_rows(mlstm_norm_w[0])), (gnw[:, 0, :], by_rows(gmlp_norm_w[0])), (gnw[:, 1, :], by_rows(gmlp_norm_b[0])),
                        (packed[0:TAPS, :], conv_w[0, :, 0:P]), (packed[TAPS:2 * TAPS, :], conv_w[0, :, P:CW]),
                        (packed[68:72, :], gmlp_bs[0]),
                        (packed[72:76, :], b_in[0, C_Q:C_Q + MLW].rearrange("(f p) -> f p", p=P)),
                        (packed[76:80, :], b_in[0, C_CA:C_CA + 2 * CW].rearrange("(f p) -> f p", p=P)),
                        (rb, by_rows(router_b))]
        small_loads += [(packed[62 + 2 * i:64 + 2 * i, :], v[0].rearrange("(f p) -> f p", p=P)) for i, v in enumerate((conv_b, conv_norm_w, conv_norm_b))]
        SMALL_LOADS = len(small_loads)

        st_full = [sem(f"stage{i}_loaded") for i in range(UNITS)]
        small_in = sem("small_loaded")
        made = sem("constants_made")
        xt_ready, xt_hi, xt_lo = sem("x_transposed"), sem("x_hi"), sem("x_lo")
        w_hi, w_lo, w_free = sem("weights_hi"), sem("weights_lo"), sem("weights_used")
        proj_done, proj_read = sem("projected"), sem("projection_read")
        act_done = sem("projection_activated")
        og_ready = sem("output_gate_ready")
        ev_out = [sem(f"spill{i}_stored") for i in range(4)]
        dve_own, act_own = sem("dve_own"), sem("act_own")
        ws_ready, ws_read = sem("ws_transposed"), sem("ws_copied")
        gv_stats, gv_rstd, z_ready, z_mixed, hb_ready, hb_out = (
            sem(n) for n in ("gv_stats", "gv_rstd", "z_ready", "z_mixed", "hb_ready", "hb_stored"))
        g_ln, g_logf, g_sums, g_u, g_uT, g_cm, g_back, g_m, g_bc, g_w, g_we, g_wk, g_nmT, g_nm, nm_out = (
            sem(n) for n in ("gate_log", "logf_ready", "gate_sums", "gate_u", "gate_u_transposed",
                             "cummax_ready", "cummax_back", "m_ready", "m_broadcast", "gate_args", "gate_weights",
                             "state_weights", "negM_transposed", "negM_rows", "negM_stored"))
        cv_sum, cv_mid, cv_sq, cv_var, cv_rstd, cv_norm, cv_done = (
            sem(n) for n in ("conv_sums", "conv_centred", "conv_squares", "conv_variance", "conv_rstd",
                             "conv_normed", "conv_branch_done"))
        k_in, q_in, v_in, nm_in, og_in, hb_in, x_in = (
            sem(n) for n in ("k_loaded", "q_loaded", "v_loaded", "negM_loaded", "gate_loaded", "hb_loaded", "x_loaded"))
        ones_col = sem("value_ones_column")
        kT_ps, kT_sb, nm_masked, e_sb, st_ps, pt_sb, ii_ps, inter_sb, num_sb, vw_sb, state_ps, c_sb = (
            sem(n) for n in ("k_transposed", "kT_copied", "negM_masked", "decays_ready", "scores_ready",
                             "weighted_scores_ready", "numerators_ready", "inter_scaled", "numerators_summed",
                             "weighted_v_ready", "state_products_ready", "state_updated"))
        h_stats, h_rstd, ha_ready, hT_ps, xr_hi, xr_lo, y_half = (
            sem(n) for n in ("head_stats", "head_rstd", "ha_ready", "h_transposed", "h_hi", "h_lo", "out_projected"))
        r_stats, r_rstd, x1_ready, x1_out, x1T_ps, x1T_sb, lg_ps, lg_read = (
            sem(n) for n in ("ln1_stats", "ln1_rstd", "x1_ready", "x1_stored", "x1_transposed", "x1T_copied",
                             "logits_ready", "logits_read"))

        ln1_in, ln2_in = sem("ln1_rows_loaded"), sem("ln2_rows_loaded")
        rt_exp, dispatch_ready, rank_ps, hot_ready, tok_ps, tok_ready = (
            sem(n) for n in ("router_exp", "dispatch_ready", "ranks_ready", "one_hots_ready", "tokens_summed", "tokens_ready"))
        xw_hi, xw_lo, xw_used = sem("expert_hi"), sem("expert_lo"), sem("expert_units_used")
        idx_ready, xe_in, xeT_ps, xe_hi, xe_lo = (
            sem(n) for n in ("tile_tokens_ready", "rows_gathered", "rows_transposed", "rows_hi", "rows_lo"))
        y_fill = sem("unused_rows_filled")
        gate_ps, up_ps, sil_sb, hid_sb, hidT_ps, hr_hi, hr_lo, y_ps, y_sb, y_out = (
            sem(n) for n in ("gate_ready", "up_ready", "silu_ready", "hidden_ready", "hidden_transposed", "hidden_hi",
                             "hidden_lo", "down_ready", "down_copied", "down_stored"))
        x1_back, y_in, stored = ([sem(f"{n}{i}") for i in range(4)] for n in ("x1_reloaded", "expert_rows_gathered", "stored"))
        x1_scaled, fin_stats, fin_rstd, scaled_ready, out_ready = (
            sem(n) for n in ("x1_scaled", "ln2_stats", "ln2_rstd", "ln2_scaled", "result_ready"))

        block = ctx.enter_context(nc.Block())

        waits_passed = sem("waits_passed")

        def wait_apart(eng, signal, count):
            eng.wait_ge(signal, count)
            eng.sem_inc(waits_passed, 1)

        def staged_unit(n):
            return stage[:, n % 8, :]

        BEFORE = [6] * 4 + [5] * 4 + [0] * 4

        def unit_source(e, u):
            if u < 8:
                return (gate_v, up_v)[u // 4][bass.ds(e, 1), :, 2 * (u % 4):2 * (u % 4) + 2, :].rearrange("e p k n -> p (e k) n")
            return down_v[bass.ds(e, 1), :, u - 8, :].rearrange("e p n -> p (e n)")

        def unit_slot(u):
            return stage[:, u, :].rearrange("p (k n) -> p k n", k=2) if u < 8 else stage[:, u, :]

        def unit_split(u, part):
            if u < 8:
                return (wg, wu)[u // 4][:, part, 2 * (u % 4):2 * (u % 4) + 2, :]
            return wd[:, part, u - 8, :]

        def wait_unit_used(eng, u, e, g):
            if u % 4 == 3:
                eng.wait_ge((gate_ps, up_ps, y_ps)[u // 4], g + 1)
            else:
                eng.wait_ge(xw_used, e * 9 + (u // 4) * 3 + u % 4 + 1)

        def each_tile(eng, regs, body, own=None):
            g_reg = eng.alloc_register(f"{regs}_tile")
            eng.reg_mov(g_reg, 0)
            if own:
                own.settle()

            def one(e, last, more):
                if own:
                    own.settle()
                body(e, eng.snap(g_reg, min_val=0, max_val=TILES_MAX - 1), last, more)
                if own:
                    own.settle()
                eng.reg_add(g_reg, g_reg, 1)

            def expert(e, more):
                extra = eng.value_load(ntiles[0:1, bass.ds(e, 1)], min_val=0, max_val=T - 1)
                with eng.If(extra > 0):
                    with eng.Fori(0, extra):
                        one(e, False, more)
                one(e, True, more)

            with eng.Fori(0, NE - 1) as i:
                expert(eng.snap(i, min_val=0, max_val=NE - 2), True)
            expert(NE - 1, False)
            if own:
                own.settle()
            return eng.snap(g_reg, min_val=NE, max_val=TILES_MAX)

        def load_unit(sp, e, u):
            sp.dma_start(unit_slot(u), unit_source(e, u)).then_inc(st_full[u], 16)

        def sp_experts(sp):
            sp.wait_ge(lg_ps, PRIMED + T)
            sp.wait_ge(x1_out, PRIMED + 16 * T)
            for u in range(8, UNITS):
                load_unit(sp, 0, u)
            sp.wait_ge(tok_ready, 1)
            tiles = sp.value_load(ntiles[0:1, NE:NE + 1], min_val=NE, max_val=TILES_MAX)
            filled = sp.alloc_register("filled")
            sp.reg_mov(filled, 0)
            with sp.Fori(tiles, TILES_MAX + 1) as i:
                j = sp.snap(i, min_val=NE, max_val=TILES_MAX)
                sp.dma_start(y_dram[bass.ds(j * P, P), :].rearrange("p (k n) -> p k n", k=KC),
                             ones[:, :].unsqueeze(1).to_broadcast([P, KC, P])).then_inc(y_fill, 16)
                sp.reg_add(filled, filled, 16)
            with sp.Fori(1, NE) as i:
                e = sp.snap(i, min_val=1, max_val=NE - 1)
                for u in range(UNITS):
                    sp.wait_ge(xw_lo, UNITS * (e - 1) + u + 1)
                    load_unit(sp, e, u)
            for t in range(T):
                if t == 0:
                    sp.wait_ge(xw_lo, UNITS * NE)
                if t >= 4:
                    sp.wait_ge(scaled_ready, t - 3)
                sp.dma_start(final(t, 2), x1_dram[t * P:(t + 1) * P, :]).then_inc(x1_back[t % 4], 16)
                if t >= 2:
                    sp.wait_ge(out_ready, t - 1)
                    sp.dma_start(out_tiles[t - 2], final(t - 2, 0)).then_inc(stored[(t - 2) % 4], 16)
            for t in range(T - 2, T):
                if t == T - 1:
                    sp.wait_ge(y_fill, sp.snap(filled))
                sp.wait_ge(out_ready, t + 1)
                sp.dma_start(out_tiles[t], final(t, 0)).then_inc(stored[t % 4], 16)
            for i in range(4):
                sp.wait_ge(stored[i], 32)


        def final(t, i):
            return stage[:, 3 * (t % 4) + i, :]

        def pool_experts(pool, own):
            def gather(j, first=False):
                if not first:
                    pool.wait_ge(xe_in, 16 * j)
                pool.tensor_copy(tok1, tok[:, bass.ds(j, 1)]).then_inc(idx_ready, 1)
                if not first:
                    pool.wait_ge(xeT_ps, j)
                if first:
                    pool.wait_ge(idx_ready, 1)
                else:
                    wait_apart(pool, idx_ready, j + 1)
                pool.indirect_dma_start(out=xe, out_offset=None, in_=x1_dram,
                                        in_offset=bass.IndirectOffsetOnAxis(ap=tok1, axis=0)).then_inc(xe_in, 16)

            pool.wait_ge(x1_out, PRIMED + 16 * T)
            pool.wait_ge(tok_ready, 1)
            gather(0, True)
            total = each_tile(pool, "pool", lambda e, g, last, more: gather(g + 1))
            pool.wait_ge(xe_in, total * 16 + 16)
            wait_apart(pool, xeT_ps, total + 1)
            for i, src in enumerate((ln2_w[0], ln2_b[0])):
                pool.dma_start(ln2[:, i, :], src.partition_broadcast(P)).then_inc(ln2_in, 16)
            pool.wait_ge(xw_lo, UNITS * NE)
            wait_apart(pool, y_out, PRIMED + total * 16)

            def fetch(t):
                if t >= 4:
                    pool.wait_ge(stored[t % 4], 16)
                for i in range(2):
                    pool.indirect_dma_start(out=final(t, i), out_offset=None, in_=y_dram,
                                            in_offset=bass.IndirectOffsetOnAxis(ap=sloti[:, i, t:t + 1], axis=0)).then_inc(y_in[t % 4], 16)

            for t in range(3):
                fetch(t)
            pool.wait_ge(ln2_in, 32)
            for t in range(T):
                if t + 3 < T:
                    fetch(t + 3)
                pool.wait_ge(scaled_ready, t + 1)
                pool.tensor_tensor(final(t, 0), final(t, 0), ln2[:, 1, :], ALU.add).then_inc(out_ready, 1)

        def pe_experts(pe):
            pe.wait_ge(dispatch_ready, 1)
            n = T * NE
            flat = disp.rearrange("p t e -> p (t e)")
            pe.matmul(bank(0)[:, 0:n], stri, flat, start=True, stop=False)
            for j in range(1, T):
                pe.matmul(bank(0)[:, j * NE:n], ones[:, :], flat[:, 0:n - j * NE], start=False, stop=(j == T - 1))
            for t in range(T):
                last = pe.matmul(bank(1)[:, 0:NE], ones[:, :], disp[:, t, :], start=(t == 0), stop=(t == T - 1))
            last.then_inc(rank_ps, 1)
            pe.wait_ge(hot_ready, 1)
            for i in range(2 * T):
                last = pe.matmul(bank(2)[:, 0:32], hot_lo[:, i, :], hot_hi[:, i, :], start=(i == 0), stop=(i == 2 * T - 1))
            last.then_inc(tok_ps, 1)

            def transpose_rows(j):
                pe.wait_ge(xe_in, j * 16 + 16)
                for k in range(KC):
                    last = pe.transpose(psum[:, 4 + k // 4, (k % 4) * P:(k % 4 + 1) * P], xe[:, k:D:KC], ident[:, :])
                last.then_inc(xeT_ps, 1)

            def body(e, g, last_tile, more):
                pe.wait_ge(xe_lo, g + 1)
                for w, b, signal, read in ((wg, 0, gate_ps, sil_sb), (wu, 1, up_ps, hid_sb)):
                    pe.wait_ge(read, PRIMED + g)
                    for k in range(KC):
                        if k % 2 == 0:
                            pe.wait_ge(xw_lo, e * UNITS + 4 * b + k // 2 + 1)
                        for i, (hx, hw) in enumerate(((0, 0), (1, 0), (0, 1))):
                            last = pe.matmul(bank(b), XR[:, hx, k, :], w[:, hw, k, :], start=(k == 0 and i == 0), stop=(k == KC - 1 and i == 2))
                        if last_tile and k % 2 == 1 and k < KC - 1:
                            last.then_inc(xw_used, 1)
                    last.then_inc(signal, 1)
                transpose_rows(g + 1)
                pe.wait_ge(hid_sb, PRIMED + g + 1)
                for f in range(FC):
                    last = pe.transpose(bank(6)[:, f * P:(f + 1) * P], hid[:, f:DE:FC], ident[:, :])
                last.then_inc(hidT_ps, 1)
                pe.wait_ge(hr_lo, g + 1)
                pe.wait_ge(y_sb, PRIMED + g)
                for f in range(FC):
                    pe.wait_ge(xw_lo, e * UNITS + 8 + f + 1)
                    for i, (hx, hw) in enumerate(((0, 0), (1, 0), (0, 1))):
                        for half in range(2):
                            last = pe.matmul(bank(2 + half), HR[:, hx, f, :], wd[:, hw, f, half * 512:half * 512 + 512],
                                             start=(f == 0 and i == 0), stop=(f == FC - 1 and i == 2))
                    if last_tile and f < FC - 1:
                        last.then_inc(xw_used, 1)
                last.then_inc(y_ps, 1)

            transpose_rows(0)
            each_tile(pe, "pe", body)

        def act_experts(act, own):
            act.wait_ge(lg_read, PRIMED + T)
            act.activation(rt[:, 0], logits, AF.Exp, scale=-1.0).then_inc(rt_exp, 1)

            def split_hi(e, u, before):
                act.wait_ge(st_full[u], (e + (BEFORE[u] + 1)) * 16)
                if before:
                    wait_unit_used(act, u, *before)
                act.activation(unit_split(u, 0), unit_slot(u), AF.Copy).then_inc(xw_hi, 1)

            act.wait_ge(y_half, 2 * T)
            for u in range(8):
                split_hi(0, u, None)

            def rows_hi(j):
                act.wait_ge(xeT_ps, j + 1)
                act.activation(XR[:, 0], psum[:, 4:6, :].rearrange("p a (k n) -> p (a k) n", n=P), AF.Copy).then_inc(xe_hi, 1)

            rows_hi(0)
            for u in range(8, UNITS):
                split_hi(0, u, None)

            def body(e, g, last_tile, more):
                split = last_tile and more
                act.wait_ge(gate_ps, g + 1)
                act.wait_ge(hid_sb, PRIMED + g)
                act.activation(sil, bank(0), AF.Silu).then_inc(sil_sb, 1)
                if split:
                    for u in range(4):
                        split_hi(e + 1, u, (e, g))
                act.wait_ge(up_ps, g + 1)
                rows_hi(g + 1)
                act.wait_ge(hidT_ps, PRIMED + g + 1)
                act.activation(HR[:, 0], bank(6).rearrange("p (f n) -> p f n", f=FC), AF.Copy).then_inc(hr_hi, 1)
                if split:
                    for u in range(4, 8):
                        split_hi(e + 1, u, (e, g))
                act.wait_ge(y_ps, g + 1)
                act.wait_ge(y_out, PRIMED + g * 16)
                act.activation(ys, psum[:, 2:4, :].rearrange("p a n -> p (a n)"), AF.Copy).then_inc(y_sb, 1)
                act.wait_ge(y_sb, PRIMED + g + 1)
                act.dma_start(y_dram[bass.ds(g * P, P), :], ys).then_inc(y_out, 16)
                if split:
                    for u in range(8, UNITS):
                        split_hi(e + 1, u, (e, g))

            each_tile(act, "act", body, own)
            for t in range(T):
                act.wait_ge(x1_back[t % 4], 16 * (t // 4 + 1))
                act.activation(final(t, 2), final(t, 2), AF.Copy, scale=ALPHA).then_inc(x1_scaled, 1)
                act.wait_ge(fin_stats, t + 1)
                own.link(act.activation(rs_f[:, t:t + 1], mv_f[:, t, 1:2], AF.Ln, bias=LN_EPS))
                act.activation(rs_f[:, t:t + 1], rs_f[:, t:t + 1], AF.Exp, scale=-0.5).then_inc(fin_rstd, 1)

        def dve_experts(dve, own):
            def rtv(i):
                return rt[:, i]

            def grp(v):
                return v.rearrange("p t (g e) -> p (t g) e", g=NG)

            def over(v, n):
                return v.unsqueeze(2).to_broadcast([P, T, n])

            dve.tensor_tensor(stri, tri[:, :], ident[:, :], ALU.subtract)
            dve.wait_ge(rt_exp, 1)
            dve.wait_ge(small_in, 16 * SMALL_LOADS)
            own.link(dve.tensor_scalar(rtv(0), rtv(0), 1.0, None, ALU.add))
            own.link(dve.reciprocal(rtv(0), rtv(0)))
            own.link(dve.tensor_tensor(rtv(1), rtv(0), rb.unsqueeze(1).to_broadcast([P, T, NE]), ALU.add))
            v = grp(rtv(1))
            dve.tensor_tensor(pairs[:, :, 0:3], v[:, :, 0:3], v[:, :, 1:4], ALU.add)
            dve.tensor_tensor(pairs[:, :, 3:5], v[:, :, 0:2], v[:, :, 2:4], ALU.add)
            own.link(dve.tensor_tensor(pairs[:, :, 5:6], v[:, :, 0:1], v[:, :, 3:4], ALU.add))
            own.link(dve.tensor_reduce(gsc.rearrange("p t g -> p (t g)"), pairs, AX.X, ALU.max))

            def first_max(dst, src, desc, n):
                own.link(dve.tensor_reduce(mx, src, AX.X, ALU.max))
                own.link(dve.tensor_tensor(dst, src, over(mx, n), ALU.is_equal))
                own.link(dve.tensor_tensor(dst, dst, desc.unsqueeze(1).to_broadcast([P, T, n]), ALU.mult))
                own.link(dve.tensor_reduce(mx, dst, AX.X, ALU.max))
                own.link(dve.tensor_tensor(dst, dst, over(mx, n), ALU.is_equal))

            first_max(gsel, gsc, i_desc[:, NE - NG:NE], NG)
            gflat = gsel.rearrange("p t g -> p (t g)")
            own.link(dve.tensor_tensor(grp(rtv(2)), grp(rtv(1)), gflat.unsqueeze(2).to_broadcast([P, T * NG, EG]), ALU.mult))
            own.link(dve.tensor_scalar(gsel, gsel, 1.0, -NEG, ALU.subtract, ALU.mult))
            own.link(dve.tensor_tensor(grp(rtv(2)), grp(rtv(2)), gflat.unsqueeze(2).to_broadcast([P, T * NG, EG]), ALU.add))
            first_max(rtv(3), rtv(2), i_desc, NE)
            own.link(dve.scalar_tensor_tensor(rtv(2), rtv(3), -3.0e38, rtv(2), ALU.mult, ALU.add))
            first_max(rtv(4), rtv(2), i_desc, NE)
            dve.tensor_tensor(disp, rtv(3), rtv(4), ALU.add).then_inc(dispatch_ready, 1)
            for i in range(2):
                own.link(dve.tensor_tensor(rtv(2), rtv(3 + i), rtv(0), ALU.mult))
                own.link(dve.tensor_reduce(gatew[:, i, :], rtv(2), AX.X, ALU.add))
            own.link(dve.tensor_tensor(mx, gatew[:, 0, :], gatew[:, 1, :], ALU.add))
            own.link(dve.reciprocal(mx, mx))
            own.link(dve.tensor_tensor(gatew, gatew, mx.unsqueeze(1).to_broadcast([P, 2, T]), ALU.mult))
            dve.wait_ge(rank_ps, 1)
            own.link(dve.tensor_copy(cnt[:, 0, :], bank(1)[:, 0:NE]))
            own.link(dve.tensor_tensor(more_than, cnt[:, 0:1, :].rearrange("p a e -> p (a e)").unsqueeze(2).to_broadcast([P, NE, T - 1]),
                                       i_thr.unsqueeze(1).to_broadcast([P, NE, T - 1]), ALU.is_gt))
            own.link(dve.tensor_reduce(cnt[:, 1, :], more_than, AX.X, ALU.add))
            dve.tensor_copy(ntiles[0:1, 0:NE], cnt[0:1, 1, :])
            own.link(dve.tensor_scalar(cnt[:, 2, :], cnt[:, 1, :], 1.0, float(P), ALU.add, ALU.mult))
            dve.memset(cnt[:, 4, :], 0.0)
            own.link(dve.memset(hot_lo[:, 0, :], 0.0))
            own.link(dve.tensor_tensor_scan(cnt[:, 3, :], cnt[:, 2, :], cnt[:, 4, :], 0.0, ALU.add, ALU.add))
            dve.tensor_scalar(ntiles[0:1, NE:NE + 1], cnt[0:1, 3, NE - 1:NE], 1.0 / P, None, ALU.mult)
            own.link(dve.tensor_tensor(cnt[:, 4, :], cnt[:, 3, :], cnt[:, 2, :], ALU.subtract))
            own.link(dve.tensor_tensor(rtv(1), bank(0)[:, 0:T * NE].rearrange("p (t e) -> p t e", t=T),
                                       cnt[:, 4:5, :].to_broadcast([P, T, NE]), ALU.add))
            for i in range(2):
                own.link(dve.tensor_tensor(rtv(2), rtv(3 + i), rtv(1), ALU.mult))
                own.link(dve.tensor_reduce(slot[:, i, :], rtv(2), AX.X, ALU.add))
            own.link(dve.tensor_copy(sloti[:, :, :], slot))
            own.link(dve.tensor_scalar(parts[:, 0], sloti[:, :, :], P - 1, None, ALU.bitwise_and))
            own.link(dve.tensor_scalar(parts[:, 1], sloti[:, :, :], 7, None, ALU.logical_shift_right))
            own.link(dve.tensor_copy(partf, parts[:, :, :, :]))
            dve.tensor_tensor(hot_lo, i_lo.unsqueeze(1).to_broadcast([P, 2 * T, P]),
                              partf[:, 0].rearrange("p a t -> p (a t)").unsqueeze(2).to_broadcast([P, 2 * T, P]), ALU.is_equal)
            own.link(dve.tensor_tensor(hot_hi, i_lo[:, 0:32].unsqueeze(1).to_broadcast([P, 2 * T, 32]),
                                       partf[:, 1].rearrange("p a t -> p (a t)").unsqueeze(2).to_broadcast([P, 2 * T, 32]), ALU.is_equal))
            for i in range(2):
                last = dve.tensor_tensor(hot_hi[:, i * T:(i + 1) * T, :], hot_hi[:, i * T:(i + 1) * T, :], over(i_tok, 32), ALU.mult)
            last.then_inc(hot_ready, 1)
            dve.wait_ge(tok_ps, 1)
            dve.tensor_copy(tok[:, :], bank(2)[:, 0:32]).then_inc(tok_ready, 1)

            def split_lo(e, u):
                dve.wait_ge(xw_hi, e * UNITS + u + 1)
                dve.tensor_tensor(unit_split(u, 1), unit_slot(u), unit_split(u, 0).bitcast(F32), ALU.subtract).then_inc(xw_lo, 1)

            def rows_lo(j):
                dve.wait_ge(xe_hi, j + 1)
                dve.tensor_tensor(XR[:, 1], psum[:, 4:6, :].rearrange("p a (k n) -> p (a k) n", n=P), XR[:, 0].bitcast(F32),
                                  ALU.subtract).then_inc(xe_lo, 1)

            for u in range(8):
                split_lo(0, u)
            rows_lo(0)
            for u in range(8, UNITS):
                split_lo(0, u)

            def body(e, g, last_tile, more):
                split = last_tile and more
                if split:
                    for u in range(4):
                        split_lo(e + 1, u)
                dve.wait_ge(up_ps, g + 1)
                dve.wait_ge(sil_sb, PRIMED + g + 1)
                dve.wait_ge(hidT_ps, PRIMED + g)
                dve.tensor_tensor(hid, sil, bank(1), ALU.mult).then_inc(hid_sb, 1)
                rows_lo(g + 1)
                dve.wait_ge(hr_hi, g + 1)
                dve.tensor_tensor(HR[:, 1], bank(6).rearrange("p (f n) -> p f n", f=FC), HR[:, 0].bitcast(F32), ALU.subtract).then_inc(hr_lo, 1)
                if split:
                    for u in range(4, UNITS):
                        split_lo(e + 1, u)

            each_tile(dve, "dve", body, own)
            for t in range(T):
                y0, y1, xr = (final(t, i) for i in range(3))
                dve.wait_ge(x1_scaled, t + 1)
                dve.wait_ge(y_in[t % 4], 32 * (t // 4 + 1))
                own.link(dve.scalar_tensor_tensor(xr, y0, gatew[:, 0, t:t + 1], xr, ALU.mult, ALU.add))
                own.link(dve.scalar_tensor_tensor(xr, y1, gatew[:, 1, t:t + 1], xr, ALU.mult, ALU.add))
                for i in range(2):
                    last = dve.bn_stats(st_c[:, i, :], xr[:, i * 512:(i + 1) * 512])
                wait_apart(dve, dve_own, own.done(last))
                dve.bn_aggr(mv_f[:, t, :], st_c).then_inc(fin_stats, 1)
                dve.wait_ge(fin_rstd, t + 1)
                own.link(dve.tensor_scalar(y1, xr, mv_f[:, t, 0:1], rs_f[:, t:t + 1], ALU.subtract, ALU.mult))
                if t == 0:
                    dve.wait_ge(ln2_in, 32)
                dve.tensor_tensor(y0, y1, ln2[:, 0, :], ALU.mult).then_inc(scaled_ready, 1)

        @block.sync
        def _(sp):
            for t in range(T):
                sp.dma_start(stage[:, t, :], x_tiles[t]).then_inc(st_full[t], 16)
            n = 0
            for c0, width in GROUPS:
                for u in range(4):
                    if n < 8:
                        sp.wait_ge(xt_ready, n + 1)
                    else:
                        sp.wait_ge(w_lo, n - 8 + 1)
                    sp.dma_start(staged_unit(n)[:, 0:2 * width].rearrange("p (k n) -> p k n", k=2),
                                 win_v[:, 2 * u:2 * u + 2, c0:c0 + width]).then_inc(st_full[n % 8], 16)
                    n += 1
            for k in range(KC):
                sp.wait_ge(w_lo, n - 8 + 1)
                sp.dma_start(staged_unit(n), wout_v[k]).then_inc(st_full[n % 8], 16)
                n += 1
            def load_kqv(c):
                sp.dma_start(kin, k_dram[bass.ds(c * P, P), :].rearrange("p (h n) -> p h n", h=HEADS)).then_inc(k_in, 16)
                sp.dma_start(qin, q_dram[:, :, bass.ds(c * P, P)]).then_inc(q_in, 16)
                sp.dma_start(vau[:, :, 0:DH], v_dram[bass.ds(c * P, P), :].rearrange("p (h n) -> p h n", h=HEADS)).then_inc(v_in, 16)

            def load_nm(c):
                sp.dma_start(nm, nm_dram[bass.ds(c * HEADS, HEADS), :].partition_broadcast(P)).then_inc(nm_in, 16)

            def load_og_hb(c):
                sp.dma_start(og, og_dram[bass.ds(c * P, P), :]).then_inc(og_in, 16)
                sp.dma_start(hbin, hb_dram[bass.ds(c * P, P), :]).then_inc(hb_in, 16)

            def load_x(c):
                sp.dma_start(xin, x[0][bass.ds(c * P, P), :]).then_inc(x_in, 16)

            def refill(c):
                sp.wait_ge(ii_ps, c)
                load_nm(c)
                sp.wait_ge(state_ps, c)
                load_kqv(c)
                sp.wait_ge(ha_ready, c)
                sp.wait_ge(hT_ps, c)
                load_og_hb(c)

            def store_x1(c):
                sp.wait_ge(x1_ready, c + 1)
                sp.dma_start(x1_dram[bass.ds(c * P, P), :], x1s).then_inc(x1_out, 16)

            sp.wait_ge(og_ready, JOBS)
            sp.wait_ge(nm_out, 16)
            sp.wait_ge(hb_out, 16)
            for i in range(4):
                sp.wait_ge(ev_out[i], 16 * 8)
            load_kqv(0)
            load_nm(0)
            load_og_hb(0)
            for i, v in enumerate((ln1_w, ln1_b)):
                sp.dma_start(ln1[:, i, :], v[0].partition_broadcast(P)).then_inc(ln1_in, 16)
            sp.dma_start(rw, router_w.rearrange("(p k) e -> p k e", k=KC)).then_inc(ln1_in, 16)
            load_x(0)
            for u in range(8):
                sp.wait_ge(w_lo, 28 + (u - 4) % 8 + 1)
                load_unit(sp, 0, u)
            refill(1)
            with sp.Fori(1, T - 1) as i:
                c = sp.snap(i, min_val=1, max_val=T - 2)
                store_x1(c - 1)
                load_x(c)
                refill(c + 1)
            store_x1(T - 2)
            load_x(T - 1)
            store_x1(T - 1)
            sp_experts(sp)

        @block.gpsimd
        def _(pool):
            own = Links(pool, sem("pool_own"), "pool_links")
            for s in (lg_read, x1_out, x1T_ps, lg_ps, sil_sb, hid_sb, y_sb, y_out, hidT_ps):
                pool.sem_inc(s, PRIMED)
            pool.memset(ones[:, :], 1.0)
            own.link(pool.memset(ident[:, :], 0.0))
            pool.affine_select(out=ident[:, :], in_=ident[:, :], compare_op=ALU.not_equal, fill=1.0, base=0,
                               pattern=[[-1, P]], channel_multiplier=1).then_inc(made, 1)
            pool.affine_select(out=tri[:, :], in_=ones[:, :], compare_op=ALU.is_ge, fill=0.0, base=0,
                               pattern=[[1, P]], channel_multiplier=-1).then_inc(made, 1)
            pool.iota(i_lo, pattern=[[1, P]], base=0, channel_multiplier=0, allow_small_or_imprecise_dtypes=True)
            pool.iota(i_desc, pattern=[[-1, NE]], base=NE, channel_multiplier=0, allow_small_or_imprecise_dtypes=True)
            pool.iota(i_thr, pattern=[[P, T - 1]], base=P, channel_multiplier=0, allow_small_or_imprecise_dtypes=True)
            own.link(pool.iota(i_tok, pattern=[[P, T]], base=0, channel_multiplier=1, allow_small_or_imprecise_dtypes=True))
            pool.wait_ge(small_in, 16 * SMALL_LOADS)
            pool.affine_select(out=wsl, in_=wsl, compare_op=ALU.is_ge, fill=0.0, base=0,
                               pattern=[[0, HEADS], [-1, P]], channel_multiplier=1).then_inc(made, 1)
            s = 0
            for g in range(3, 7):
                for j in range(JOBS):
                    if g < 6:
                        pool.wait_ge(proj_read, g * JOBS + j + 1)
                    else:
                        pool.wait_ge(og_ready, j + 1)
                    if g == 3:
                        dst = q_dram[:, j // 2, (j % 2) * 512:(j % 2) * 512 + 512]
                    else:
                        dst = (k_dram, v_dram, og_dram)[g - 4][j * P:(j + 1) * P, :]
                    pool.dma_start(dst, ev[:, s % 4, :]).then_inc(ev_out[s % 4], 16)
                    s += 1
                if g == 5:
                    pool.wait_ge(hb_ready, 4)
                    pool.dma_start(hb_dram.rearrange("(t p) n -> p t n", p=P), ug).then_inc(hb_out, 16)
            pool.wait_ge(g_nm, 1)
            pool.dma_start(nm_dram, gT[0:NC_, 2, :]).then_inc(nm_out, 16)
            for i in range(4):
                pool.wait_ge(ev_out[i], 16 * 8)
            pool.wait_ge(hb_out, 16)
            pool.wait_ge(og_ready, JOBS)
            own.link(pool.memset(nmask, 0.0))
            own.link(pool.affine_select(out=nmask, in_=nmask, compare_op=ALU.is_ge, fill=NEG, base=0,
                                        pattern=[[1, P]], channel_multiplier=-1))
            pool.memset(vau[:, :, DH:DH + 1], 1.0).then_inc(ones_col, 1)

            def weigh(c):
                pool.wait_ge(nm_in, 16 * c + 16)
                pool.tensor_tensor(nm, nm, nmask.unsqueeze(1).to_broadcast([P, HEADS, P]), ALU.add).then_inc(nm_masked, 1)
                pool.wait_ge(v_in, 16 * c + 16)
                pool.wait_ge(ones_col, 1)
                pool.wait_ge(st_ps, c + 1)
                pool.tensor_tensor(vw, vau, w4[:, 0, bass.ds(c * HEADS, HEADS)].unsqueeze(2).to_broadcast([P, HEADS, DH + 1]),
                                   ALU.mult).then_inc(vw_sb, 1)

            weigh(0)
            with pool.Fori(1, T) as i:
                weigh(pool.snap(i, min_val=1, max_val=T - 1))
            pool_experts(pool, own)

        @block.tensor
        def _(pe):
            pe.wait_ge(made, 2)
            for t in range(T):
                pe.wait_ge(st_full[t], 16)
                if t >= 2:
                    pe.wait_ge(xt_lo, t - 1)
                b = 4 + 2 * (t % 2)
                for k in range(KC):
                    last = pe.transpose(psum[:, b + k // 4, (k % 4) * P:(k % 4 + 1) * P], stage[:, t, k:D:KC], ident[:, :])
                last.then_inc(xt_ready, 1)
            pe.wait_ge(made, 3)
            pe.wait_ge(xt_lo, T)
            for h in range(HEADS):
                pe.transpose(bank(4)[:, h * P:(h + 1) * P], wsl[:, h, :], ident[:, :])
            pe.wait_ge(small_in, 16 * SMALL_LOADS)
            pe.transpose(bank(5)[:, 0:80], packed, ident[0:80, 0:80]).then_inc(ws_ready, 1)

            def group(g, width, features, turn=0, first=False):
                for j in range(JOBS):
                    if not (first and j < 4):
                        pe.wait_ge(proj_read, g * JOBS + j - 3)
                    b = bank(j % 4)
                    for k in range(KC):
                        if j == 0 and k % 2 == 0:
                            pe.wait_ge(w_lo, g * 4 + k // 2 + 1)
                        for i, (hx, hw) in enumerate(((0, 0), (1, 0), (0, 1))):
                            if features:
                                f, half = (j // 2 + turn) % 4, j % 2
                                last = pe.matmul(b, wc[:, hw, k, f * P:(f + 1) * P], xT[:, hx, k, half * 512:half * 512 + 512],
                                                 start=(k == 0 and i == 0), stop=(k == KC - 1 and i == 2))
                            else:
                                last = pe.matmul(b[:, 0:width], xT[:, hx, k, j * P:(j + 1) * P], wc[:, hw, k, 0:width],
                                                 start=(k == 0 and i == 0), stop=(k == KC - 1 and i == 2))
                        if j == JOBS - 1 and k % 2 == 1 and k < KC - 1:
                            last.then_inc(w_free, 1)
                    last.then_inc(proj_done, 1)

            group(0, GROUPS[0][1], False, first=True)
            group(1, GROUPS[1][1], False)
            pe.wait_ge(g_logf, 1)
            pe.matmul(bank(5)[:, 0:NC_], tri[:, :], gt[:, 2, :], start=True, stop=True)
            pe.matmul(bank(5)[:, NC_:2 * NC_], ones[:, :], gt[:, 2, :], start=True, stop=True).then_inc(g_sums, 1)
            group(2, GROUPS[2][1], True, turn=2)
            pe.wait_ge(g_u, 1)
            pe.transpose(bank(5)[0:NC_, 128:256], uS, ident[:, :])
            pe.transpose(bank(5)[0:NC_, 256:384], gt[:, 6, :], ident[:, :]).then_inc(g_uT, 1)
            group(3, GROUPS[3][1], True)
            pe.wait_ge(g_cm, 1)
            pe.transpose(bank(5)[:, 384:384 + NC_], gT[0:NC_, 0, :], ident[0:NC_, 0:NC_])
            pe.transpose(bank(5)[0:1, 448:448 + NC_], gT[0:NC_, 1, 0:1], ident[0:NC_, 0:NC_]).then_inc(g_back, 1)
            pe.wait_ge(z_ready, 1)
            pe.wait_ge(ws_read, 1)
            for h in range(HEADS - 1):
                pe.matmul(bank((4, 6, 7)[h]), wsT[:, h, :], gvs[:, :, h * GHD:(h + 1) * GHD], start=True, stop=True).then_inc(z_mixed, 1)
            group(4, GROUPS[4][1], False)
            pe.wait_ge(hb_ready, 1)
            pe.matmul(bank(4), wsT[:, HEADS - 1, :], gvs[:, :, (HEADS - 1) * GHD:HEADS * GHD], start=True, stop=True).then_inc(z_mixed, 1)
            pe.wait_ge(g_m, 1)
            pe.matmul(bank(5)[:, 64:64 + 2 * NC_], ones[0:1, :], grow[0:1, 1:3, :], start=True, stop=True).then_inc(g_bc, 1)
            with pe.Fori(5, 7) as i:
                group(pe.snap(i, min_val=5, max_val=6), MLW, False)
            pe.wait_ge(g_w, 1)
            pe.transpose(bank(5)[0:NC_, 0:P], gt[:, 0, :], ident[:, :]).then_inc(g_nmT, 1)
            def channel_sums(src, signal):
                for half in range(2):
                    for f in range(2):
                        last = pe.matmul(bank(6 + half), ones[:, :], src[:, f, half * 512:half * 512 + 512], start=(f == 0), stop=(f == 1))
                last.then_inc(signal, 1)

            pe.wait_ge(og_ready, JOBS)
            pe.wait_ge(hb_ready, 4)
            channel_sums(acc, cv_sum)
            pe.wait_ge(cv_sq, 1)
            channel_sums(gvs.rearrange("p t n -> p (t n)").rearrange("p (f n) -> p f n", f=2), cv_var)

            def transpose_k(c):
                pe.wait_ge(k_in, 16 * c + 16)
                pe.wait_ge(xr_lo, c)
                for h in range(HEADS):
                    last = pe.transpose(bank(0)[:, h * P:(h + 1) * P], kin[:, h, :], ident[:, :])
                last.then_inc(kT_ps, 1)

            def scores(c):
                pe.wait_ge(q_in, 16 * c + 16)
                pe.wait_ge(kT_sb, c + 1)
                for h in range(HEADS):
                    last = pe.matmul(bank(1)[:, h * P:(h + 1) * P], kT[:, h, :], qin[:, h, :], start=True, stop=True)
                last.then_inc(st_ps, 1)

            def numerators(c):
                pe.wait_ge(v_in, 16 * c + 16)
                pe.wait_ge(ones_col, 1)
                pe.wait_ge(pt_sb, c + 1)
                pe.wait_ge(c_sb, c + 1)
                for h in range(HEADS):
                    o = (h % 2) * (DH + 1)
                    pe.matmul(psum[:, 2 + h // 2, o:o + DH + 1], nm[:, h, :], vau[:, h, :], start=True, stop=True)
                    last = pe.matmul(psum[:, 4 + h // 2, o:o + DH + 1], qin[:, h, :], C[:, h, :], start=True, stop=True)
                last.then_inc(ii_ps, 1)

            def state_products(c):
                pe.wait_ge(vw_sb, c + 1)
                pe.wait_ge(inter_sb, c + 1)
                for h in range(HEADS):
                    o = (h % 2) * (DH + 1)
                    last = pe.matmul(psum[:, 4 + h // 2, o:o + DH + 1], kin[:, h, :], vw[:, h, :], start=True, stop=True)
                last.then_inc(state_ps, 1)

            def out_projection(c, half):
                if half == 0:
                    pe.wait_ge(xr_lo, c + 1)
                    pe.wait_ge(lg_read, PRIMED + c)
                for k in range(KC):
                    for i, (hx, hw) in enumerate(((0, 0), (1, 0), (0, 1))):
                        last = pe.matmul(bank(6 + half), XR[:, hx, k, :], wo[:, hw, k, half * 512:half * 512 + 512],
                                         start=(k == 0 and i == 0), stop=(k == KC - 1 and i == 2))
                last.then_inc(y_half, 1)

            def route(c, summed):
                pe.wait_ge(ln1_in, 48)
                pe.wait_ge(x1_ready, c + 1)
                pe.wait_ge(num_sb, summed)
                for k in range(KC):
                    last = pe.transpose(psum[:, 2 + k // 4, (k % 4) * P:(k % 4 + 1) * P], x1s[:, k:D:KC], ident[:, :])
                last.then_inc(x1T_ps, 1)
                pe.wait_ge(x1T_sb, c + 1)
                for k in range(KC):
                    last = pe.matmul(bank(6)[:, 0:NE], x1T[:, k * P:(k + 1) * P], rw[:, k, :], start=(k == 0), stop=(k == KC - 1))
                last.then_inc(lg_ps, 1)

            def transpose_h(c):
                pe.wait_ge(ha_ready, c + 1)
                pe.wait_ge(hb_in, 16 * c + 16)
                for h in range(HEADS):
                    pe.transpose(bank(0)[:, h * P:(h + 1) * P], ha[:, h, :], ident[:, :])
                for k in range(2):
                    last = pe.transpose(bank(1)[:, k * P:(k + 1) * P], hbin[:, k * P:(k + 1) * P], ident[:, :])
                last.then_inc(hT_ps, 1)

            pe.wait_ge(proj_read, 7 * JOBS)
            transpose_k(0)
            scores(0)
            numerators(0)
            state_products(0)
            transpose_h(0)
            pe.wait_ge(w_lo, 28 + KC)
            with pe.Fori(1, T) as i:
                c = pe.snap(i, min_val=1, max_val=T - 1)
                transpose_k(c)
                out_projection(c - 1, 0)
                scores(c)
                out_projection(c - 1, 1)
                numerators(c)
                state_products(c)
                route(c - 1, c + 1)
                transpose_h(c)
            out_projection(T - 1, 0)
            out_projection(T - 1, 1)
            route(T - 1, T)
            pe_experts(pe)

        @block.scalar
        def _(act):
            own = Links(act, act_own, "act_links")
            for dst, src in small_loads:
                act.dma_start(dst, src).then_inc(small_in, 16)

            for t in range(T):
                act.wait_ge(xt_ready, t + 1)
                b = 4 + 2 * (t % 2)
                act.activation(xT[:, 0, :, t * P:(t + 1) * P], psum[:, b:b + 2, :].rearrange("p a (k n) -> p (a k) n", n=P),
                               AF.Copy).then_inc(xt_hi, 1)

            def split_hi(g, u):
                n, width = 4 * g + u, GROUPS[g][1]
                act.wait_ge(st_full[n % 8], 16 * (n // 8 + 2))
                if g and u < 3:
                    act.wait_ge(w_free, 3 * (g - 1) + u + 1)
                elif g:
                    act.wait_ge(proj_done, JOBS * g)
                act.activation(wc[:, 0, 2 * u:2 * u + 2, 0:width],
                               staged_unit(n)[:, 0:2 * width].rearrange("p (k n) -> p k n", k=2), AF.Copy).then_inc(w_hi, 1)

            for u in range(4):
                split_hi(0, u)
            for g in range(2):
                for t in range(T):
                    if t == T - 1:
                        for u in range(4):
                            split_hi(g + 1, u)
                    act.wait_ge(proj_read, g * JOBS + t + 1)
                    act.activation((ug, gvs)[g][:, t, :], ev[:, t % 2, 0:GW], AF.Gelu_apprx_tanh).then_inc(act_done, 1)
                if g == 0:
                    own.link(act.activation(gt[:, 0, :].rearrange("p (t h) -> p t h", t=T), gates[:, :, HEADS:2 * HEADS], AF.Abs))
                    own.link(act.activation(gt[:, 0, :], gt[:, 0, :], AF.Exp, scale=-1.0))
                    act.activation(gt[:, 1, :], gt[:, 0, :], AF.Ln, bias=1.0).then_inc(g_ln, 1)
            for j in range(4):
                act.wait_ge(proj_read, 2 * JOBS + j + 1)
                v = acc[:, j // 2, (j % 2) * 512:(j % 2) * 512 + 512]
                act.activation(v, v, AF.Sigmoid).then_inc(act_done, 1)
            act.wait_ge(gv_stats, 1)
            own.link(act.activation(rs_a, mv_a[:, :, 1], AF.Ln, bias=LN_EPS))
            act.activation(rs_a, rs_a, AF.Exp, scale=-0.5).then_inc(gv_rstd, 1)
            for u in range(4):
                split_hi(3, u)
            for g in range(4, 7):
                for u in range(4):
                    split_hi(g, u)
            act.wait_ge(g_w, 1)
            act.activation(w4, w4, AF.Exp).then_inc(g_we, 1)
            for j in range(JOBS):
                if j == JOBS - 1:
                    for k in range(KC):
                        n = 28 + k
                        act.wait_ge(st_full[n % 8], 16 * (n // 8 + 2))
                        if k < 6:
                            act.wait_ge(w_free, 3 * 6 + k // 2 + 1)
                        else:
                            act.wait_ge(proj_done, JOBS * 7)
                        act.activation(wo[:, 0, k, :], staged_unit(n), AF.Copy).then_inc(w_hi, 1)
                act.wait_ge(proj_read, 6 * JOBS + j + 1)
                act.activation(ev[:, j % 4, :], ev[:, j % 4, :], AF.Sigmoid).then_inc(act_done, 1)
            act.wait_ge(g_nmT, 1)
            act.activation(gT[0:NC_, 2, :], bank(5)[0:NC_, 0:P], AF.Copy).then_inc(g_nm, 1)
            cv = gvs.rearrange("p t n -> p (t n)").rearrange("p (f n) -> p f n", f=2)
            act.wait_ge(cv_mid, 1)
            act.activation(cv, acc, AF.Square).then_inc(cv_sq, 1)
            act.wait_ge(cv_var, 1)
            own.link(act.activation(cv[:, 0, :], psum[:, 6:8, :].rearrange("p a n -> p (a n)"), AF.Ln, scale=1.0 / CW, bias=LN_EPS))
            act.activation(cv[:, 0, :], cv[:, 0, :], AF.Exp, scale=-0.5).then_inc(cv_rstd, 1)
            act.wait_ge(cv_norm, 1)
            for f in range(2):
                last = act.activation(acc[:, f, :], acc[:, f, :], AF.Silu, scale=convc[:, 1, f:f + 1], bias=convc[:, 2, f:f + 1])
            last.then_inc(cv_done, 1)

            def copy_kT(c):
                act.wait_ge(kT_ps, c + 1)
                act.wait_ge(state_ps, c)
                act.activation(kT, bank(0).rearrange("p (h n) -> p h n", h=HEADS), AF.Copy).then_inc(kT_sb, 1)

            def decays(c):
                act.wait_ge(nm_masked, c + 1)
                for h in range(HEADS):
                    last = act.activation(nm[:, h, :], nm[:, h, :], AF.Exp, bias=uS[:, bass.ds(c * HEADS + h, 1)])
                last.then_inc(e_sb, 1)

            def scale_inter(c):
                act.wait_ge(ii_ps, c + 1)
                act.wait_ge(ha_ready, c)
                for h in range(HEADS):
                    o = (h % 2) * (DH + 1)
                    last = act.activation(num[:, h, :], psum[:, 4 + h // 2, o:o + DH + 1], AF.Copy,
                                          scale=w4[:, 2, bass.ds(c * HEADS + h, 1)])
                last.then_inc(inter_sb, 1)

            def rstd(dst, var, eps, stats, count, signal):
                act.wait_ge(stats, count)
                own.link(act.activation(dst, var, AF.Ln, bias=eps))
                act.activation(dst, dst, AF.Exp, scale=-0.5).then_inc(signal, 1)

            def copy_x1T(c):
                act.wait_ge(x1T_ps, PRIMED + c + 1)
                act.wait_ge(lg_ps, PRIMED + c)
                act.activation(x1T, psum[:, 2:4, :].rearrange("p a n -> p (a n)"), AF.Copy).then_inc(x1T_sb, 1)

            def split_h(c):
                act.wait_ge(hT_ps, c + 1)
                act.wait_ge(y_half, 2 * c)
                act.activation(XR[:, 0, 0:4, :], bank(0).rearrange("p (h n) -> p h n", h=HEADS), AF.Copy)
                act.activation(XR[:, 0, 4:6, :], bank(1)[:, 0:256].rearrange("p (h n) -> p h n", h=2), AF.Copy)
                act.activation(XR[:, 0, 6:8, :], acc[:, :, bass.ds(c * P, P)], AF.Copy).then_inc(xr_hi, 1)

            copy_kT(0)
            decays(0)
            scale_inter(0)
            rstd(rs_b, mv_b[:, :, 1], ML_EPS, h_stats, 1, h_rstd)
            split_h(0)
            own.settle()
            with act.Fori(1, T) as i:
                own.settle()
                c = act.snap(i, min_val=1, max_val=T - 1)
                copy_kT(c)
                decays(c)
                rstd(rs_c, mv_c[:, 1:2], LN_EPS, r_stats, c, r_rstd)
                scale_inter(c)
                rstd(rs_b, mv_b[:, :, 1], ML_EPS, h_stats, c + 1, h_rstd)
                copy_x1T(c - 1)
                split_h(c)
                own.settle()
            own.settle()
            rstd(rs_c, mv_c[:, 1:2], LN_EPS, r_stats, T, r_rstd)
            copy_x1T(T - 1)
            act_experts(act, own)

        @block.vector
        def _(dve):
            own = Links(dve, dve_own, "dve_links")
            dve.memset(cpad[:, :, 0:TAPS - 1], 0.0)
            own.link(dve.memset(gT[:, 2, :], 0.0))
            for t in range(T):
                dve.wait_ge(xt_hi, t + 1)
                b = 4 + 2 * (t % 2)
                dve.tensor_tensor(xT[:, 1, :, t * P:(t + 1) * P], psum[:, b:b + 2, :].rearrange("p a (k n) -> p (a k) n", n=P),
                                  xT[:, 0, :, t * P:(t + 1) * P].bitcast(F32), ALU.subtract).then_inc(xt_lo, 1)

            def split_lo(g, u):
                n, width = 4 * g + u, GROUPS[g][1]
                dve.wait_ge(w_hi, n + 1)
                dve.tensor_tensor(wc[:, 1, 2 * u:2 * u + 2, 0:width],
                                  staged_unit(n)[:, 0:2 * width].rearrange("p (k n) -> p k n", k=2),
                                  wc[:, 0, 2 * u:2 * u + 2, 0:width].bitcast(F32), ALU.subtract).then_inc(w_lo, 1)

            for u in range(4):
                split_lo(0, u)
            dve.wait_ge(ws_ready, 1)
            own.link(dve.tensor_copy(cols, bank(5)[:, 0:80]))
            dve.tensor_copy(wsT, bank(4).rearrange("p (h n) -> p h n", h=HEADS)).then_inc(ws_read, 1)
            dve.wait_ge(small_in, 16 * SMALL_LOADS)

            f_pre, i_pre = gates[:, :, HEADS:2 * HEADS], gates[:, :, 0:HEADS]

            def tab(r):
                return gt[:, r, :].rearrange("p (t h) -> p t h", t=T)

            for g in range(2):
                for t in range(T):
                    if t == T - 1:
                        for u in range(4):
                            split_lo(g + 1, u)
                    n = g * JOBS + t
                    dve.wait_ge(proj_done, n + 1)
                    o = 0
                    if g == 0:
                        o = 2 * HEADS
                        dve.tensor_tensor(gates[:, t, :], bank(t % 4)[:, 0:o], b_tm[:, 0, 0:o], ALU.add)
                    if n >= 2:
                        dve.wait_ge(act_done, n - 1)
                    dve.tensor_tensor(ev[:, t % 2, 0:GW], bank(t % 4)[:, o:o + GW], b_tm[:, g, o:o + GW], ALU.add).then_inc(proj_read, 1)
                    if g == 1 and t == 3:
                        dve.wait_ge(g_ln, 1)
                        dve.scalar_tensor_tensor(tab(2), f_pre, 0.0, tab(1), ALU.min, ALU.subtract).then_inc(g_logf, 1)

            def gv_statistics():
                for t in range(T):
                    dve.wait_ge(act_done, T + t + 1)
                    own.link(dve.bn_stats(st_a[:, t, :], gvs[:, t, :]))
                    last = dve.bn_aggr(mv_a[:, t, :], st_a[:, t, :])
                last.then_inc(gv_stats, 1)

            def gate_sums():
                dve.wait_ge(g_sums, 1)
                dve.tensor_copy(gt[:, 3, :], bank(5)[:, 0:NC_])
                own.link(dve.tensor_copy(gt[:, 4, :], bank(5)[:, NC_:2 * NC_]))
                own.link(dve.tensor_tensor(uS.rearrange("p (t h) -> p t h", t=T), i_pre, tab(3), ALU.subtract))
                dve.tensor_tensor(gt[:, 6, :], gt[:, 4, :], uS, ALU.add).then_inc(g_u, 1)

            for j in range(JOBS):
                if j == JOBS - 1:
                    for u in range(4):
                        split_lo(3, u)
                n = 2 * JOBS + j
                f, half = (j // 2 + 2) % 4, j % 2
                dve.wait_ge(proj_done, n + 1)
                if f >= 2:
                    dve.tensor_scalar(acc[:, f - 2, half * 512:half * 512 + 512], bank(j % 4), bq_fm[:, 4 + f:5 + f], None,
                                      ALU.add).then_inc(proj_read, 1)
                else:
                    dve.wait_ge(act_done, 2 * T + 4)
                    dve.scalar_tensor_tensor(cpad[:, f, TAPS - 1 + half * 512:TAPS - 1 + half * 512 + 512], bank(j % 4),
                                             bq_fm[:, 4 + f:5 + f], acc[:, f, half * 512:half * 512 + 512],
                                             ALU.add, ALU.mult).then_inc(proj_read, 1)
                if j == 0:
                    gv_statistics()
                if j == 2:
                    gate_sums()

            def tap(i):
                for f in range(2):
                    if i == 0:
                        last = dve.tensor_scalar(acc[:, f, :], cpad[:, f, 0:SEQ], convw[:, f, 0:1], convc[:, 0, f:f + 1], ALU.mult, ALU.add)
                    else:
                        last = dve.scalar_tensor_tensor(acc[:, f, :], cpad[:, f, i:i + SEQ], convw[:, f, i:i + 1], acc[:, f, :],
                                                        ALU.mult, ALU.add)
                return own.done(last)

            dve.wait_ge(proj_read, 3 * JOBS)
            tapped = tap(0)

            def z_norm():
                dve.wait_ge(gv_rstd, 1)
                for t in range(T):
                    last = dve.tensor_scalar(gvs[:, t, :], gvs[:, t, :], mv_a[:, t, 0:1], rs_a[:, t:t + 1], ALU.subtract, ALU.mult)
                own.link(last)
                own.link(dve.tensor_tensor(gvs, gvs, gnw[:, 0:1, :].to_broadcast([P, T, GW]), ALU.mult))
                dve.tensor_tensor(gvs, gvs, gnw[:, 1:2, :].to_broadcast([P, T, GW]), ALU.add).then_inc(z_ready, 1)

            def cummax():
                dve.wait_ge(g_uT, 1)
                own.link(dve.tensor_tensor_scan(gT[0:NC_, 0, :], gT[0:NC_, 2, :], bank(5)[0:NC_, 128:256], -3.0e38, ALU.add, ALU.max))
                dve.tensor_reduce(gT[0:NC_, 1, 0:1], bank(5)[0:NC_, 256:384], AX.X, ALU.max).then_inc(g_cm, 1)

            def m_scan():
                dve.wait_ge(g_back, 1)
                dve.tensor_copy(gt[:, 7, :], bank(5)[:, 384:384 + NC_])
                dve.memset(grow[0:1, 2, 0:HEADS], 0.0)
                own.link(dve.tensor_copy(grow[0:1, 0, :], bank(5)[0:1, 448:448 + NC_]))
                for h in range(HEADS):
                    last = dve.tensor_tensor_scan(grow[0:1, 1, h:NC_:HEADS], gt[0:1, 4, h:NC_:HEADS], grow[0:1, 0, h:NC_:HEADS], 0.0,
                                                  ALU.add, ALU.max)
                own.link(last)
                dve.tensor_copy(grow[0:1, 2, HEADS:NC_], grow[0:1, 1, 0:NC_ - HEADS]).then_inc(g_m, 1)

            def mix_z(h):
                dve.wait_ge(z_mixed, h + 1)
                v = ug[:, :, h * GHD:(h + 1) * GHD]
                dve.scalar_tensor_tensor(v, bank((4, 6, 7, 4)[h]).rearrange("p (t n) -> p t n", t=T), bs_col[:, h:h + 1], v,
                                         ALU.add, ALU.mult).then_inc(hb_ready, 1)

            def gate_args():
                dve.wait_ge(g_bc, 1)
                own.link(dve.tensor_copy(gt[:, 8:10, :], bank(5)[:, 64:64 + 2 * NC_].rearrange("p (a n) -> p a n", a=2)))
                own.link(dve.tensor_tensor(gt[:, 7, :], gt[:, 9, :], gt[:, 7, :], ALU.max))
                dve.tensor_tensor(w4[:, 0, :], gt[:, 6, :], gt[:, 8, :], ALU.subtract)
                own.link(dve.tensor_tensor(gt[:, 5, :], gt[:, 4, :], gt[:, 9, :], ALU.add))
                dve.tensor_tensor(w4[:, 1, :], gt[:, 5, :], gt[:, 8, :], ALU.subtract)
                dve.tensor_tensor(w4[:, 2, :], gt[:, 9, :], gt[:, 7, :], ALU.subtract)
                dve.scalar_tensor_tensor(w4[:, 3, :], gt[:, 3, :], -1.0, gt[:, 7, :], ALU.mult, ALU.subtract)
                dve.tensor_scalar(gt[:, 0, :], gt[:, 7, :], -1.0, None, ALU.mult).then_inc(g_w, 1)

            def weigh_og(j):
                s = j % 4
                dve.wait_ge(act_done, 2 * T + 4 + j + 1)
                dve.tensor_tensor(ev[:, s, :], ev[:, s, :], mlw, ALU.mult).then_inc(og_ready, 1)

            s = 0
            for g in range(3, 7):
                for j in range(JOBS):
                    n = g * JOBS + j
                    if j == JOBS - 1 and g < 6:
                        for u in range(4):
                            split_lo(g + 1, u)
                    if j == JOBS - 1 and g == 6:
                        for k in range(KC):
                            dve.wait_ge(w_hi, 28 + k + 1)
                            dve.tensor_tensor(wo[:, 1, k, :], staged_unit(28 + k), wo[:, 0, k, :].bitcast(F32), ALU.subtract).then_inc(w_lo, 1)
                    dve.wait_ge(proj_done, n + 1)
                    if s >= 4:
                        dve.wait_ge(ev_out[s % 4], 16 * (s // 4))
                    if g == 3:
                        dve.tensor_scalar(ev[:, s % 4, :], bank(j % 4), bq_fm[:, j // 2:j // 2 + 1], None, ALU.add).then_inc(proj_read, 1)
                    else:
                        dve.tensor_tensor(ev[:, s % 4, :], bank(j % 4), b_tm[:, g - 2, :], ALU.add).then_inc(proj_read, 1)
                    s += 1
                    i = 1 + (g - 3) * JOBS + j
                    if i < TAPS:
                        dve.wait_ge(dve_own, tapped)
                        tapped = tap(i)
                    if g == 3 and j == 0:
                        z_norm()
                    if g == 3 and j == 3:
                        cummax()
                    if g == 4 and j < 3:
                        mix_z(j)
                    if g == 4 and j == 3:
                        m_scan()
                    if g == 5 and j == 0:
                        mix_z(3)
                    if g == 5 and j == 1:
                        gate_args()
                    if g == 6 and j == 3:
                        dve.wait_ge(g_we, 1)
                        dve.tensor_scalar(w4[:, 0, :], w4[:, 0, :], KSCALE, None, ALU.mult).then_inc(g_wk, 1)
                    if g == 6 and j >= 1:
                        weigh_og(j - 1)
            weigh_og(JOBS - 1)
            dve.wait_ge(cv_sum, 1)
            for f in range(2):
                last = dve.scalar_tensor_tensor(acc[:, f, :], psum[:, 6:8, :].rearrange("p a n -> p (a n)"), -1.0 / CW, acc[:, f, :],
                                                ALU.mult, ALU.add)
            last.then_inc(cv_mid, 1)
            cvr = gvs.rearrange("p t n -> p (t n)").rearrange("p (f n) -> p f n", f=2)
            dve.wait_ge(cv_rstd, 1)
            for f in range(2):
                last = dve.tensor_tensor(acc[:, f, :], acc[:, f, :], cvr[:, 0, :], ALU.mult)
            last.then_inc(cv_norm, 1)

            dve.wait_ge(g_nm, 1)
            dve.wait_ge(nm_out, 16)
            dve.wait_ge(hb_out, 16)
            for i in range(4):
                dve.wait_ge(ev_out[i], 16 * 8)
            dve.memset(C, 0.0).then_inc(c_sb, 1)
            dve.wait_ge(c_sb, 1)

            def weigh_scores(c):
                dve.wait_ge(e_sb, c + 1)
                dve.wait_ge(st_ps, c + 1)
                dve.scalar_tensor_tensor(nm, bank(1).rearrange("p (h n) -> p h n", h=HEADS), KSCALE, nm, ALU.mult, ALU.mult).then_inc(pt_sb, 1)

            def residual1(c):
                dve.wait_ge(x_in, 16 * c + 16)
                dve.wait_ge(y_half, 2 * c + 2)
                own.link(dve.scalar_tensor_tensor(xin, xin, ALPHA, psum[:, 6:8, :].rearrange("p a n -> p (a n)"), ALU.mult, ALU.add))
                for i in range(2):
                    last = dve.bn_stats(st_c[:, i, :], xin[:, i * 512:(i + 1) * 512])
                wait_apart(dve, dve_own, own.done(last))
                dve.bn_aggr(mv_c, st_c).then_inc(r_stats, 1)

            def norm1(c):
                dve.wait_ge(ln1_in, 48)
                dve.wait_ge(r_rstd, c + 1)
                own.link(dve.tensor_scalar(xin, xin, mv_c[:, 0:1], rs_c, ALU.subtract, ALU.mult))
                own.link(dve.tensor_tensor(xin, xin, ln1[:, 0, :], ALU.mult))
                dve.wait_ge(x1_out, PRIMED + 16 * c)
                dve.wait_ge(x1T_ps, PRIMED + c)
                dve.tensor_tensor(x1s, xin, ln1[:, 1, :], ALU.add).then_inc(x1_ready, 1)

            def sum_numerators(c):
                dve.wait_ge(inter_sb, c + 1)
                for i in range(2):
                    v = num[:, 2 * i:2 * i + 2, :]
                    last = dve.tensor_tensor(v, psum[:, 2 + i, 0:2 * (DH + 1)].rearrange("p (h n) -> p h n", h=2), v, ALU.add)
                last.then_inc(num_sb, 1)

            def update_state(c):
                dve.wait_ge(state_ps, c + 1)
                for h in range(HEADS):
                    o = (h % 2) * (DH + 1)
                    last = dve.scalar_tensor_tensor(C[:, h, :], C[:, h, :], w4[:, 1, bass.ds(c * HEADS + h, 1)],
                                                    psum[:, 4 + h // 2, o:o + DH + 1], ALU.mult, ALU.add)
                last.then_inc(c_sb, 1)

            def divide(c):
                dve.wait_ge(num_sb, c + 1)
                d = num[:, :, DH:DH + 1]
                own.link(dve.scalar_tensor_tensor(den.unsqueeze(2), d, -1.0, d, ALU.mult, ALU.max))
                own.link(dve.tensor_tensor(den, den, w4[:, 3, bass.ds(c * HEADS, HEADS)], ALU.max))
                own.link(dve.reciprocal(den, den))
                dve.wait_ge(hT_ps, c)
                own.link(dve.tensor_tensor(ha, num[:, :, 0:DH], den.unsqueeze(2).to_broadcast([P, HEADS, DH]), ALU.mult))
                for h in range(HEADS):
                    last = dve.bn_stats(st_b[:, h, :], ha[:, h, :])
                wait_apart(dve, dve_own, own.done(last))
                for h in range(HEADS):
                    last = dve.bn_aggr(mv_b[:, h, :], st_b[:, h, :])
                last.then_inc(h_stats, 1)

            def finish_h(c):
                dve.wait_ge(h_rstd, c + 1)
                for h in range(HEADS):
                    last = dve.tensor_scalar(ha[:, h, :], ha[:, h, :], mv_b[:, h, 0:1], rs_b[:, h:h + 1], ALU.subtract, ALU.mult)
                own.link(last)
                dve.wait_ge(og_in, 16 * c + 16)
                dve.tensor_tensor(ha, ha, og.rearrange("p (h n) -> p h n", h=HEADS), ALU.mult).then_inc(ha_ready, 1)

            def read_logits(c):
                dve.wait_ge(lg_ps, PRIMED + c + 1)
                dve.tensor_copy(logits[:, bass.ds(c, 1), :], bank(6)[:, 0:NE].unsqueeze(1)).then_inc(lg_read, 1)

            def split_h(c):
                dve.wait_ge(xr_hi, c + 1)
                for v, src in ((slice(0, 4), bank(0).rearrange("p (h n) -> p h n", h=HEADS)),
                               (slice(4, 6), bank(1)[:, 0:256].rearrange("p (h n) -> p h n", h=2)),
                               (slice(6, 8), acc[:, :, bass.ds(c * P, P)])):
                    last = dve.tensor_tensor(XR[:, 1, v, :], src, XR[:, 0, v, :].bitcast(F32), ALU.subtract)
                last.then_inc(xr_lo, 1)

            weigh_scores(0)
            sum_numerators(0)
            update_state(0)
            divide(0)
            finish_h(0)
            dve.wait_ge(cv_done, 1)
            split_h(0)
            own.settle()
            with dve.Fori(1, T) as i:
                own.settle()
                c = dve.snap(i, min_val=1, max_val=T - 1)
                weigh_scores(c)
                residual1(c - 1)
                sum_numerators(c)
                update_state(c)
                norm1(c - 1)
                divide(c)
                finish_h(c)
                read_logits(c - 1)
                split_h(c)
                own.settle()
            own.settle()
            residual1(T - 1)
            norm1(T - 1)
            read_logits(T - 1)
            dve_experts(dve, own)


_INS = ["x", "w_in", "b_in", "mlstm_norm_w", "gmlp_norm_w", "gmlp_norm_b", "gmlp_ws", "gmlp_bs", "conv_w", "conv_b",
        "conv_norm_w", "conv_norm_b", "w_out", "ln1_w", "ln1_b", "router_w", "router_b", "w_gate", "w_up", "w_down",
        "ln2_w", "ln2_b"]


def kernel(**inputs):
    import concourse.bacc as bacc
    from concourse.bass_utils import run_bass_kernel_spmd

    nc = bacc.Bacc("TRN2", target_bir_lowering=False, num_devices=1)
    arrays, args = {}, []
    for name in _INS:
        a = np.ascontiguousarray(inputs[name])
        arrays[f"in_{name}"] = a
        args.append(nc.dram_tensor(f"in_{name}", a.shape, mybir.dt.from_np(a.dtype), kind="ExternalInput").ap())
    args.append(nc.dram_tensor("out_dram", (1, SEQ, D), F32, kind="ExternalOutput").ap())
    hybrid_kernel(nc, *args)
    r = run_bass_kernel_spmd(nc, [arrays], core_ids=[0])
    return r.results[0]["out_dram"]
```

```python
from contextlib import ExitStack

import concourse.bass as bass
import numpy as np
from concourse import mybir

F32 = mybir.dt.float32
F32R = mybir.dt.float32r
I32 = mybir.dt.int32
BF16 = mybir.dt.bfloat16
ALU = mybir.AluOpType
AF = mybir.ActivationFunctionType
AX = mybir.AxisListType

P = 128
D = 1024
SEQ = 1024
KC = D // P
T = SEQ // P
HEADS = 4
DH = 128
MLW = HEADS * DH
GW = 256
GHD = GW // HEADS
CW = 256
TAPS = 31
NE = 16
NG = 4
EG = NE // NG
DE = 512
FC = DE // P
ALPHA = 2.0 ** 0.25
LN_EPS = 1e-5
ML_EPS = 1e-6
KSCALE = DH ** -0.5
GELU_IN = HEADS * 2
NEG = -1.0e30
TILES_MAX = (2 * SEQ + NE * (P - 1)) // P
SMALL = 1136
UNITS = 12

C_Q, C_K, C_V, C_O, C_GATE = 0, MLW, 2 * MLW, 3 * MLW, 4 * MLW
C_GU = C_GATE + 2 * HEADS
C_GV = C_GU + GW
C_CA = C_GV + GW
C_CB = C_CA + CW
GROUPS = [(C_GATE, 2 * HEADS + GW), (C_GV, GW), (C_CA, 2 * CW), (C_Q, MLW), (C_K, MLW), (C_V, MLW), (C_O, MLW)]
SETS = 5
JOBS = 8

DH2 = DE // 2
PASSES = ((0, 0), (1, 0), (0, 1))

PRIMED = 1


class Chunk:

    def __init__(self, c, n, r):
        self.c, self.n, self.r, self.b = c, n, r, n % 2

    def plus(self, d):
        n = self.n + d
        return Chunk(self.c + d, n, self.r + (n // 2 - self.n // 2))


def chunk_steps(eng, step, own=None):
    def settled(c, n, r):
        if own:
            own.settle()
        step(Chunk(c, n, r))
        if own:
            own.settle()

    for c in range(2):
        settled(c, c, c // 2)
    with eng.Fori(1, T // 2 - 1) as i:
        r = eng.snap(i, min_val=1, max_val=T // 2 - 2)
        c = eng.snap(r * 2, min_val=2, max_val=T - 4)
        settled(c, 2, r)
        settled(c + 1, 3, r)
    for c in range(T - 2, T + 2):
        settled(c, c, c // 2)


class Links:

    def __init__(self, eng, sem, name):
        self.eng, self.sem, self.n = eng, sem, 0
        self.reg = eng.alloc_register(name)
        eng.reg_mov(self.reg, 0)
        self.base = 0

    def done(self, ins):
        self.n += 1
        ins.then_inc(self.sem, 1)
        return self.base + self.n

    def link(self, ins):
        self.eng.wait_ge(self.sem, self.done(ins))

    def settle(self):
        if self.n:
            self.eng.reg_add(self.reg, self.reg, self.n)
        self.n = 0
        self.base = self.eng.snap(self.reg)


def hybrid_kernel(nc, x, w_in, b_in, mlstm_norm_w, gmlp_norm_w, gmlp_norm_b, gmlp_ws, gmlp_bs,
                  conv_w, conv_b, conv_norm_w, conv_norm_b, w_out, ln1_w, ln1_b, router_w, router_b,
                  w_gate, w_up, w_down, ln2_w, ln2_b, out):
    ctx = ExitStack()
    with ctx:
        def sb(name, shape, dt=F32):
            return ctx.enter_context(nc.sbuf_tensor(name, shape, dt))

        def sem(name):
            return ctx.enter_context(nc.semaphore(name))

        def dram(name, shape, dt=F32):
            return nc.dram_tensor(name, shape, dt, kind="Internal").ap()

        x_tiles = x[0].rearrange("(t p) n -> t p n", p=P)
        out_tiles = out[0].rearrange("(t p) n -> t p n", p=P)
        win_v = w_in[0].rearrange("(p k) n -> p k n", k=KC)
        wout_v = w_out[0].rearrange("(k p) n -> k p n", p=P)
        gate_v = w_gate[0].rearrange("e (p k) n -> e p k n", k=KC)
        up_v = w_up[0].rearrange("e (p k) n -> e p k n", k=KC)
        down_v = w_down[0].rearrange("e (a p f) n -> e p a f n", a=2, p=P)

        k_dram = dram("k_scratch", (SEQ, MLW))
        v_dram = dram("v_scratch", (SEQ, MLW))
        og_dram = dram("og_scratch", (SEQ, MLW))
        hb_dram = dram("hb_scratch", (SEQ, GW))
        q_dram = dram("q_scratch", (P, HEADS, SEQ))
        nm_dram = dram("nm_scratch", (T * HEADS, P))
        x1_dram = dram("x1_scratch", (SEQ, D))
        y_dram = dram("y_scratch", ((TILES_MAX + 1) * P, D))

        WR = sb("split_weights", [P, 24576], F32R)
        XR = sb("split_rows", [P, 2, KC, P], F32R)
        HR = sb("split_hidden", [P, 2, FC, P], F32R)
        xT = WR[:, 0:16384].rearrange("p (h k n) -> p h k n", h=2, k=KC)
        wc = WR[:, 16384:24576].rearrange("p (h k n) -> p h k n", h=2, k=KC)
        wo = xT
        wg = wc
        wu = WR[:, 0:8192].rearrange("p (h k n) -> p h k n", h=2, k=KC)
        wd = WR[:, 8192:16384].rearrange("p (h k n) -> p h k n", h=2, k=FC)

        arena = sb("arena", [P, 12352 + 2048])
        stage = arena[:, 0:12288].rearrange("p (s n) -> p s n", s=UNITS)
        cpad = arena[:, 8192:8192 + 2 * 1056].rearrange("p (f n) -> p f n", f=2)
        gvs = arena[:, 10304:10304 + 2048].rearrange("p (t n) -> p t n", t=T)
        acc = arena[:, 12352:14400].rearrange("p (f n) -> p f n", f=2)
        rows = arena[:, 8192:12288].rearrange("p (s n) -> p s n", s=4)
        NF = 9130
        work = sb("work", [P, NF])
        used = {"a": 0, "b": 0, "c": 0, "d": 0}

        def at(phase, *shape):
            n = int(np.prod(shape))
            o = used[phase]
            used[phase] = o + n
            assert used[phase] <= NF, (phase, used[phase])
            v = work[:, o:o + n]
            if len(shape) == 2:
                v = v.rearrange("p (a b) -> p a b", a=shape[0])
            elif len(shape) == 3:
                v = v.rearrange("p (a b c) -> p a b c", a=shape[0], b=shape[1])
            return v

        ident = sb("ident", [P, P])
        tri = sb("tri", [P, P])
        ones = sb("ones", [P, P])
        small = sb("small", [P, SMALL])
        small_used = [0]

        def sm(*shape):
            n = int(np.prod(shape))
            o = small_used[0]
            small_used[0] = o + n
            assert o + n <= SMALL, o + n
            v = small[:, o:o + n]
            if len(shape) == 2:
                v = v.rearrange("p (a b) -> p a b", a=shape[0])
            elif len(shape) == 3:
                v = v.rearrange("p (a b c) -> p a b c", a=shape[0], b=shape[1])
            return v

        NC_ = T * HEADS
        uS = sm(NC_)
        w4 = sm(4, NC_)
        logits = sm(T, NE)
        cols = sm(80)
        convw = cols[:, 0:2 * TAPS].rearrange("p (f j) -> p f j", f=2)
        convc = cols[:, 2 * TAPS:2 * TAPS + 6].rearrange("p (i f) -> p i f", i=3)
        bs_col = cols[:, 68:72]
        bq_fm = cols[:, 72:80]
        slot = sm(2, T)
        gatew = sm(2, T)
        st_a = sm(T, 6)
        mv_a = sm(T, 2)
        rs_a = sm(T)
        st_b = sm(HEADS, 6)
        mv_b = sm(HEADS, 2)
        rs_b = sm(HEADS)
        den = sm(HEADS)
        st_c = sm(2, 6)
        mv_c = sm(2)
        rs_c = sm(1)
        mv_f = sm(T, 2)
        rs_f = sm(T)
        shift_f = sm(T)
        rb = sm(NE)
        i_lo = sm(P)
        i_desc = sm(NE)
        i_thr = sm(T - 1)
        i_tok = sm(T)
        tok1 = sb("tile_tokens", [P, 1], I32)[:, :]
        parts = sb("slot_parts", [P, 2, 2, T], I32)
        sloti = sb("slot_index", [P, 2, T], I32)
        tok = sb("token_index", [P, 32], I32)
        ntiles = sb("extra_tiles", [1, 3], I32)
        place = sm(NE // 2)



        b_tm = at("a", 5, 512)
        mlw = at("a", MLW)
        gnw = at("a", 2, GW)
        wsT = at("a", HEADS, P)
        ev = at("a", 4, 512)
        ug = at("a", T, GW)
        gates = at("a", T, 2 * HEADS)
        wsl = ev[:, 2, :].rearrange("p (h n) -> p h n", h=HEADS)
        packed = ev[0:80, 3, 0:P]
        gt = at("a", 10, NC_)
        gT = at("a", 3, P)
        grow = at("a", 5, NC_)
        spare = arena[:, 4096:8192]
        halves = lambda v: v.rearrange("p (h n) -> p h n", h=HEADS)
        XRb = [XR, WR[:, 16384:16384 + 2 * KC * P].rearrange("p (h k n) -> p h k n", h=2, k=KC)]

        def halves(v):
            return v.rearrange("p (h n) -> p h n", h=HEADS)

        kT = at("b", HEADS, P)
        vw = at("b", HEADS, DH + 1)
        num = at("b", HEADS, DH + 1)
        hb0 = at("b", GW)
        nmask = at("b", P)
        used["b"] = 4 * 512
        og0 = at("b", HEADS, DH)
        ha = at("b", HEADS, DH)
        C = at("b", HEADS, DH + 1)
        rw = at("b", KC, NE)
        used["b"] = 5 * 512 + MLW + 2 * GW + HEADS * P
        ln1 = at("b", 2, D)
        kin = [at("b", HEADS, DH), halves(spare[:, 0:MLW])]
        qin = [at("b", HEADS, P), halves(spare[:, MLW:2 * MLW])]
        nm = [at("b", HEADS, P), halves(spare[:, 2 * MLW:3 * MLW])]
        vau = [at("b", HEADS, DH + 1), halves(spare[:, 2304:2304 + HEADS * (DH + 1)])]
        og = [og0, halves(spare[:, 3 * MLW:4 * MLW])]
        hbin = [hb0, spare[:, 4 * MLW:4 * MLW + GW]]
        xin = [rows[:, 0], rows[:, 3]]
        x1s, x1T = rows[:, 1], rows[:, 2]
        rt = work[:, 0:5 * T * NE].rearrange("p (i t e) -> p i t e", i=5, t=T)
        used["c"] = 5 * T * NE
        whole = arena[:, 12352:14400].bitcast(BF16)
        hot_lo = whole[:, 0:2 * T * P].rearrange("p (i n) -> p i n", n=P)
        hot_hi = whole[:, 2 * T * P:2 * T * (P + 64)].rearrange("p (i n) -> p i n", n=64)
        disp = whole[:, 2 * T * (P + 64):2 * T * (P + 64) + T * NE].rearrange("p (t e) -> p t e", t=T)
        ones_bf = whole[:, 2 * T * (P + 64) + T * NE:2 * T * (P + 64) + T * NE + P]
        stri = whole[:, 2 * T * (P + 64) + T * NE + P:2 * T * (P + 64) + T * NE + 2 * P]
        pairs = at("c", T * NG, 6)
        gsc = at("c", T, NG)
        gsel = at("c", T, NG)
        mx = at("c", T)
        cnt = at("c", 5, NE)
        more_than = at("c", NE, T - 1)
        partf = at("c", 2, 2, T)
        hot_tile = at("c", 2 * T, 32)
        tok_sum = at("c", 64)
        packing = at("c", 2, NE // 2)[0:1]
        packed_sum = at("c", 2)[0:1]
        xe = at("d", D)
        sil = at("d", DE)
        hid = at("d", DE)
        ys = at("d", D)
        ln2 = at("d", 2, D)
        last_rows = at("d", D)
        psum = ctx.enter_context(nc.psum_tensor("banks", [P, 8, 512], F32))

        def bank(i):
            return psum[:, i, :]

        def by_rows(v):
            return v.partition_broadcast(P)

        small_loads = [(b_tm[:, i, 0:w], by_rows(b_in[0, c:c + w])) for i, (c, w) in
                       enumerate(((C_GATE, 2 * HEADS + GW), (C_GV, GW), (C_K, MLW), (C_V, MLW), (C_O, MLW)))]
        small_loads += [(wsl, gmlp_ws[0].rearrange("h t s -> t h s")),
                        (mlw, by_rows(mlstm_norm_w[0])), (gnw[:, 0, :], by_rows(gmlp_norm_w[0])), (gnw[:, 1, :], by_rows(gmlp_norm_b[0])),
                        (packed[0:TAPS, :], conv_w[0, :, 0:P]), (packed[TAPS:2 * TAPS, :], conv_w[0, :, P:CW]),
                        (packed[68:72, :], gmlp_bs[0]),
                        (packed[72:76, :], b_in[0, C_Q:C_Q + MLW].rearrange("(f p) -> f p", p=P)),
                        (packed[76:80, :], b_in[0, C_CA:C_CA + 2 * CW].rearrange("(f p) -> f p", p=P)),
                        (rb, by_rows(router_b))]
        small_loads += [(packed[62 + 2 * i:64 + 2 * i, :], v[0].rearrange("(f p) -> f p", p=P)) for i, v in enumerate((conv_b, conv_norm_w, conv_norm_b))]
        SMALL_LOADS = len(small_loads)

        st_full = [sem(f"stage{i}_loaded") for i in range(UNITS)]
        small_in = sem("small_loaded")
        made = sem("constants_made")
        xt_ready, xt_hi, xt_lo = sem("x_transposed"), sem("x_hi"), sem("x_lo")
        w_hi, w_lo, w_free = sem("weights_hi"), sem("weights_lo"), sem("weights_used")
        proj_done, proj_read = sem("projected"), sem("projection_read")
        act_done = sem("projection_activated")
        og_ready = sem("output_gate_ready")
        ev_out = [sem(f"spill{i}_stored") for i in range(4)]
        dve_own, act_own = sem("dve_own"), sem("act_own")
        ws_ready, ws_read = sem("ws_transposed"), sem("ws_copied")
        gv_stats, gv_rstd, z_ready, z_mixed, hb_ready, hb_out = (
            sem(n) for n in ("gv_stats", "gv_rstd", "z_ready", "z_mixed", "hb_ready", "hb_stored"))
        g_ln, g_logf, g_sums, g_u, g_uT, g_cm, g_back, g_m, g_bc, g_w, g_we, g_wk, g_nmT, g_nm, nm_out = (
            sem(n) for n in ("gate_log", "logf_ready", "gate_sums", "gate_u", "gate_u_transposed",
                             "cummax_ready", "cummax_back", "m_ready", "m_broadcast", "gate_args", "gate_weights",
                             "state_weights", "negM_transposed", "negM_rows", "negM_stored"))
        cv_sum, cv_mid, cv_sq, cv_var, cv_rstd, cv_norm, cv_done = (
            sem(n) for n in ("conv_sums", "conv_centred", "conv_squares", "conv_variance", "conv_rstd",
                             "conv_normed", "conv_branch_done"))
        kq_in, v_in, nm_in, og_hb_in, x_in = (
            [sem(f"{n}_loaded{b}") for b in range(2)] for n in ("kq", "v", "negM", "gate_hb", "x"))
        fin_std, fin_norm = sem("ln2_deviation"), sem("ln2_normed")
        y_summed, taps_done = sem("out_projection_summed"), sem("taps_done")
        ones_col = sem("value_ones_column")
        kT_ps, kT_sb, nm_masked, e_sb, st_ps, pt_sb, ii_ps, inter_sb, num_sb, vw_sb, state_ps, c_sb = (
            sem(n) for n in ("k_transposed", "kT_copied", "negM_masked", "decays_ready", "scores_ready",
                             "weighted_scores_ready", "numerators_ready", "inter_scaled", "numerators_summed",
                             "weighted_v_ready", "state_products_ready", "state_updated"))
        h_stats, h_std, ha_ready, hT_ps, xr_hi, xr_lo, y_half = (
            sem(n) for n in ("head_stats", "head_deviation", "ha_ready", "h_transposed", "h_hi", "h_lo", "out_projected"))
        r_stats, r_std, x1_ready, x1_out, x1T_ps, x1T_sb, lg_ps, lg_read = (
            sem(n) for n in ("ln1_stats", "ln1_deviation", "x1_ready", "x1_stored", "x1_transposed", "x1T_copied",
                             "logits_ready", "logits_read"))

        ln1_in, ln2_in = sem("ln1_rows_loaded"), sem("ln2_rows_loaded")
        rt_exp, dispatch_ready, rank_ps, hot_ready, tok_ps, tok_ready = (
            sem(n) for n in ("router_exp", "dispatch_ready", "ranks_ready", "one_hots_ready", "tokens_summed", "tokens_ready"))
        xw_hi, xw_lo, xw_used = sem("expert_hi"), sem("expert_lo"), sem("expert_units_used")
        idx_ready, xe_in, xeT_ps, xe_hi, xe_lo = (
            sem(n) for n in ("tile_tokens_ready", "rows_gathered", "rows_transposed", "rows_hi", "rows_lo"))
        y_fill = sem("unused_rows_filled")
        gate_ps, up_ps, sil_sb, hid_sb, hidT_ps, hr_hi, hr_lo, y_ps, y_sb, y_out = (
            sem(n) for n in ("gate_ready", "up_ready", "silu_ready", "hidden_ready", "hidden_transposed", "hidden_hi",
                             "hidden_lo", "down_ready", "down_copied", "down_stored"))
        x1_back, y_in, stored = ([sem(f"{n}{i}") for i in range(SETS)] for n in ("x1_reloaded", "expert_rows_gathered", "stored"))
        x1_scaled, fin_stats, fin_rstd, scaled_ready, out_ready = (
            sem(n) for n in ("x1_scaled", "ln2_stats", "ln2_rstd", "ln2_scaled", "result_ready"))

        block = ctx.enter_context(nc.Block())

        waits_passed = sem("waits_passed")

        def wait_apart(eng, signal, count):
            eng.wait_ge(signal, count)
            eng.sem_inc(waits_passed, 1)

        def staged_unit(n):
            return stage[:, n % 8, :]

        up_bank, hidT_bank = (1, 7), (6, 0)
        WORD = T ** (NE // 2) - 1
        BEFORE = [6] * 4 + [5] * 4 + [0] * 4

        def unit_source(e, u):
            if u < 8:
                return (gate_v, up_v)[u // 4][bass.ds(e, 1), :, 2 * (u % 4):2 * (u % 4) + 2, :].rearrange("e p k n -> p (e k) n")
            a, f = divmod(u - 8, 2)
            return down_v[bass.ds(e, 1), :, a, f, :].rearrange("e p n -> p (e n)")

        def unit_slot(u):
            return stage[:, u, :].rearrange("p (k n) -> p k n", k=2) if u < 8 else stage[:, u, :]

        def unit_split(u, part):
            if u < 8:
                return (wg, wu)[u // 4][:, part, 2 * (u % 4):2 * (u % 4) + 2, :]
            return wd[:, part, u - 8, :]

        def wait_unit_used(eng, u, e, g):
            if u % 4 == 3:
                eng.wait_ge((gate_ps, up_ps, y_ps)[u // 4], (2 * g + 2) if u // 4 == 1 else (g + 1))
            else:
                eng.wait_ge(xw_used, e * 9 + (u // 4) * 3 + u % 4 + 1)

        def each_tile(eng, regs, body, own=None):
            g_reg, low, high = (eng.alloc_register(f"{regs}_{n}") for n in ("tile", "counts", "later_counts"))
            eng.reg_mov(g_reg, 0)
            for i, reg in enumerate((low, high)):
                eng.reg_mov(reg, eng.value_load(ntiles[0:1, i:i + 1], min_val=0, max_val=WORD))
            if own:
                own.settle()

            def one(e, last, more):
                if own:
                    own.settle()
                body(e, eng.snap(g_reg, min_val=0, max_val=TILES_MAX - 1), last, more)
                if own:
                    own.settle()
                eng.reg_add(g_reg, g_reg, 1)

            def expert(e, more):
                extra = eng.snap(eng.snap(low) & (T - 1), min_val=0, max_val=T - 1)
                eng.reg_mov(low, (eng.snap(low) >> 3) + ((eng.snap(high) & (T - 1)) << 21))
                eng.reg_mov(high, eng.snap(high) >> 3)
                with eng.If(extra > 0):
                    with eng.Fori(0, extra):
                        one(e, False, more)
                one(e, True, more)

            with eng.Fori(0, NE - 1) as i:
                expert(eng.snap(i, min_val=0, max_val=NE - 2), True)
            expert(NE - 1, False)
            if own:
                own.settle()
            return eng.snap(g_reg, min_val=NE, max_val=TILES_MAX)

        def load_unit(sp, e, u):
            sp.dma_start(unit_slot(u), unit_source(e, u)).then_inc(st_full[u], 16)

        def sp_experts(sp):
            sp.wait_ge(hT_ps, T)
            for u in range(8):
                load_unit(sp, 0, u)
            sp.wait_ge(lg_ps, PRIMED + T)
            sp.wait_ge(x1_out, PRIMED + 16 * T)
            for u in range(8, UNITS):
                load_unit(sp, 0, u)
            sp.wait_ge(tok_ready, 1)
            tiles = sp.value_load(ntiles[0:1, 2:3], min_val=NE, max_val=TILES_MAX)
            filled = sp.alloc_register("filled")
            sp.reg_mov(filled, 0)
            with sp.Fori(tiles, TILES_MAX + 1) as i:
                j = sp.snap(i, min_val=NE, max_val=TILES_MAX)
                sp.dma_start(y_dram[bass.ds(j * P, P), :].rearrange("p (k n) -> p k n", k=KC),
                             ones[:, :].unsqueeze(1).to_broadcast([P, KC, P])).then_inc(y_fill, 16)
                sp.reg_add(filled, filled, 16)
            with sp.Fori(1, NE) as i:
                e = sp.snap(i, min_val=1, max_val=NE - 1)
                for u in range(UNITS):
                    sp.wait_ge(xw_lo, UNITS * (e - 1) + u + 1)
                    load_unit(sp, e, u)
            def reload_x1(t):
                sp.dma_start(final(t, 2), x1_dram[t * P:(t + 1) * P, :]).then_inc(x1_back[t % SETS], 16)

            sp.wait_ge(xw_lo, UNITS * NE)
            for t in range(SETS):
                reload_x1(t)
            for t in range(T):
                if t == T - 1:
                    sp.wait_ge(y_fill, sp.snap(filled))
                sp.wait_ge(out_ready, t + 1)
                sp.dma_start(out_tiles[t], final(t, 0)).then_inc(stored[t % SETS], 16)
                if t + SETS < T:
                    reload_x1(t + SETS)
            for i in range(SETS):
                sp.wait_ge(stored[i], 16 * len(range(i, T, SETS)))


        def final(t, i):
            n = 3 * (t % SETS) + i
            return arena[:, n * D:(n + 1) * D] if n < 14 else last_rows

        def pool_experts(pool, own):
            def gather(j, first=False):
                if not first:
                    pool.wait_ge(xe_in, 16 * j)
                pool.tensor_copy(tok1, tok[:, bass.ds(j, 1)]).then_inc(idx_ready, 1)
                if not first:
                    pool.wait_ge(xeT_ps, j)
                if first:
                    pool.wait_ge(idx_ready, 1)
                else:
                    wait_apart(pool, idx_ready, j + 1)
                pool.indirect_dma_start(out=xe, out_offset=None, in_=x1_dram,
                                        in_offset=bass.IndirectOffsetOnAxis(ap=tok1, axis=0)).then_inc(xe_in, 16)

            pool.wait_ge(x1_out, PRIMED + 16 * T)
            pool.wait_ge(tok_ready, 1)
            gather(0, True)
            total = each_tile(pool, "pool", lambda e, g, last, more: gather(g + 1))
            pool.wait_ge(xe_in, total * 16 + 16)
            wait_apart(pool, xeT_ps, total + 1)
            for i, src in enumerate((ln2_w[0], ln2_b[0])):
                pool.dma_start(ln2[:, i, :], src.partition_broadcast(P)).then_inc(ln2_in, 16)
            pool.wait_ge(xw_lo, UNITS * NE)
            wait_apart(pool, y_out, PRIMED + total * 16)

            def fetch(t):
                if t >= SETS:
                    pool.wait_ge(stored[t % SETS], 16)
                for i in range(2):
                    pool.indirect_dma_start(out=final(t, i), out_offset=None, in_=y_dram,
                                            in_offset=bass.IndirectOffsetOnAxis(ap=sloti[:, i, t:t + 1], axis=0)).then_inc(y_in[t % SETS], 16)

            for t in range(3):
                fetch(t)
            pool.wait_ge(ln2_in, 32)
            for t in range(T):
                if t + 3 < T:
                    fetch(t + 3)
                pool.wait_ge(scaled_ready, t + 1)
                pool.tensor_tensor(final(t, 0), final(t, 0), ln2[:, 1, :], ALU.add).then_inc(out_ready, 1)

        def pe_experts(pe):
            pe.wait_ge(dispatch_ready, 1)
            n = T * NE
            flat = disp.rearrange("p t e -> p (t e)")
            pe.matmul(bank(0)[:, 0:n], stri, flat, start=True, stop=False)
            for j in range(1, T):
                pe.matmul(bank(0)[:, j * NE:n], ones_bf, flat[:, 0:n - j * NE], start=False, stop=(j == T - 1))
            for t in range(T):
                last = pe.matmul(bank(1)[:, 0:NE], ones_bf, disp[:, t, :], start=(t == 0), stop=(t == T - 1))
            last.then_inc(rank_ps, 1)
            pe.wait_ge(hot_ready, 1)
            for i in range(2 * T):
                last = pe.matmul(bank(2)[:, 0:64], hot_lo[:, i, :], hot_hi[:, i, :], start=(i == 0), stop=(i == 2 * T - 1))
            last.then_inc(tok_ps, 1)

            def transpose_rows(j):
                pe.wait_ge(xe_in, j * 16 + 16)
                for k in range(KC):
                    last = pe.transpose(psum[:, 4 + k // 4, (k % 4) * P:(k % 4 + 1) * P], xe[:, k:D:KC], ident[:, :])
                last.then_inc(xeT_ps, 1)

            def transpose_hidden(g, a):
                pe.wait_ge(hid_sb, 2 * g + a + 1)
                for f in range(2):
                    last = pe.transpose(bank(hidT_bank[a])[:, f * P:(f + 1) * P], hid[:, a * DH2 + f:(a + 1) * DH2:2], ident[:, :])
                last.then_inc(hidT_ps, 1)

            def body(e, g, last_tile, more):
                pe.wait_ge(xe_lo, g + 1)
                for k in range(KC):
                    if k % 2 == 0:
                        pe.wait_ge(xw_lo, e * UNITS + k // 2 + 1)
                    for i, (hx, hw) in enumerate(PASSES):
                        last = pe.matmul(bank(0), XR[:, hx, k, :], wg[:, hw, k, :], start=(k == 0 and i == 0), stop=(k == KC - 1 and i == 2))
                    if last_tile and k % 2 == 1 and k < KC - 1:
                        last.then_inc(xw_used, 1)
                last.then_inc(gate_ps, 1)
                for a in range(2):
                    for k in range(KC):
                        if a == 0 and k % 2 == 0:
                            pe.wait_ge(xw_lo, e * UNITS + 4 + k // 2 + 1)
                        if a == 1 and k == KC // 2:
                            transpose_hidden(g, 0)
                        for i, (hx, hw) in enumerate(PASSES):
                            last = pe.matmul(bank(up_bank[a])[:, 0:DH2], XR[:, hx, k, :], wu[:, hw, k, a * DH2:(a + 1) * DH2],
                                             start=(k == 0 and i == 0), stop=(k == KC - 1 and i == 2))
                        if a == 1 and last_tile and k % 2 == 1 and k < KC - 1:
                            last.then_inc(xw_used, 1)
                    last.then_inc(up_ps, 1)
                transpose_rows(g + 1)
                transpose_hidden(g, 1)
                pe.wait_ge(y_sb, PRIMED + g)
                for f in range(FC):
                    if f % 2 == 0:
                        pe.wait_ge(hr_lo, 2 * g + f // 2 + 1)
                    pe.wait_ge(xw_lo, e * UNITS + 8 + f + 1)
                    for i, (hx, hw) in enumerate(PASSES):
                        for half in range(2):
                            last = pe.matmul(bank(2 + half), HR[:, hx, f, :], wd[:, hw, f, half * 512:half * 512 + 512],
                                             start=(f == 0 and i == 0), stop=(f == FC - 1 and i == 2))
                    if last_tile and f < FC - 1:
                        last.then_inc(xw_used, 1)
                last.then_inc(y_ps, 1)

            transpose_rows(0)
            each_tile(pe, "pe", body)

        def act_experts(act, own):
            act.wait_ge(lg_read, PRIMED + T)
            act.activation(rt[:, 0], logits, AF.Exp, scale=-1.0).then_inc(rt_exp, 1)

            def split_hi(e, u, before):
                act.wait_ge(st_full[u], (e + (BEFORE[u] + 1)) * 16)
                if before:
                    wait_unit_used(act, u, *before)
                act.activation(unit_split(u, 0), unit_slot(u), AF.Copy).then_inc(xw_hi, 1)

            act.wait_ge(y_half, 2 * T)
            for u in range(8):
                split_hi(0, u, None)

            def rows_hi(j):
                act.wait_ge(xeT_ps, j + 1)
                act.activation(XR[:, 0], psum[:, 4:6, :].rearrange("p a (k n) -> p (a k) n", n=P), AF.Copy).then_inc(xe_hi, 1)

            rows_hi(0)
            for u in range(8, UNITS):
                split_hi(0, u, None)

            def hidden_hi(g, a):
                act.wait_ge(hidT_ps, 2 * g + a + 1)
                act.activation(HR[:, 0, 2 * a:2 * a + 2], bank(hidT_bank[a])[:, 0:DH2].rearrange("p (f n) -> p f n", f=2), AF.Copy).then_inc(hr_hi, 1)

            def body(e, g, last_tile, more):
                def split(*units):
                    if last_tile and more:
                        for u in units:
                            split_hi(e + 1, u, (e, g))

                act.wait_ge(gate_ps, g + 1)
                act.activation(sil, bank(0), AF.Silu).then_inc(sil_sb, 1)
                split(0, 1, 2)
                hidden_hi(g, 0)
                split(3)
                hidden_hi(g, 1)
                act.wait_ge(up_ps, 2 * g + 2)
                rows_hi(g + 1)
                split(4, 5, 6)
                act.wait_ge(y_ps, g + 1)
                act.wait_ge(y_out, PRIMED + g * 16)
                act.activation(ys, psum[:, 2:4, :].rearrange("p a n -> p (a n)"), AF.Copy).then_inc(y_sb, 1)
                act.wait_ge(y_sb, PRIMED + g + 1)
                act.dma_start(y_dram[bass.ds(g * P, P), :], ys).then_inc(y_out, 16)
                split(7, 8, 9, 10, 11)

            each_tile(act, "act", body, own)
            def scale_x1(t):
                act.wait_ge(x1_back[t % SETS], 16 * (t // SETS + 1))
                act.activation(final(t, 2), final(t, 2), AF.Copy, scale=ALPHA).then_inc(x1_scaled, 1)

            scale_x1(0)
            scale_x1(1)
            for t in range(T):
                act.wait_ge(fin_stats, t + 1)
                act.activation(rs_f[:, t:t + 1], mv_f[:, t, 1:2], AF.Sqrt, bias=LN_EPS).then_inc(fin_std, 1)
                if t + 2 < T:
                    scale_x1(t + 2)
                act.wait_ge(fin_rstd, t + 1)
                act.activation(final(t, 1), final(t, 2), AF.Identity, scale=rs_f[:, t:t + 1], bias=shift_f[:, t:t + 1]).then_inc(fin_norm, 1)

        def dve_experts(dve, own):
            def rtv(i):
                return rt[:, i]

            def grp(v):
                return v.rearrange("p t (g e) -> p (t g) e", g=NG)

            def over(v, n):
                return v.unsqueeze(2).to_broadcast([P, T, n])

            dve.tensor_copy(ones_bf, ones[:, :])
            dve.tensor_tensor(stri, tri[:, :], ident[:, :], ALU.subtract)
            dve.wait_ge(rt_exp, 1)
            dve.wait_ge(small_in, 16 * SMALL_LOADS)
            own.link(dve.tensor_scalar(rtv(0), rtv(0), 1.0, None, ALU.add))
            own.link(dve.reciprocal(rtv(0), rtv(0)))
            own.link(dve.tensor_tensor(rtv(1), rtv(0), rb.unsqueeze(1).to_broadcast([P, T, NE]), ALU.add))
            v = grp(rtv(1))
            dve.tensor_tensor(pairs[:, :, 0:3], v[:, :, 0:3], v[:, :, 1:4], ALU.add)
            dve.tensor_tensor(pairs[:, :, 3:5], v[:, :, 0:2], v[:, :, 2:4], ALU.add)
            own.link(dve.tensor_tensor(pairs[:, :, 5:6], v[:, :, 0:1], v[:, :, 3:4], ALU.add))
            own.link(dve.tensor_reduce(gsc.rearrange("p t g -> p (t g)"), pairs, AX.X, ALU.max))

            def first_max(dst, src, desc, n):
                own.link(dve.tensor_reduce(mx, src, AX.X, ALU.max))
                own.link(dve.tensor_tensor(dst, src, over(mx, n), ALU.is_equal))
                own.link(dve.tensor_tensor(dst, dst, desc.unsqueeze(1).to_broadcast([P, T, n]), ALU.mult))
                own.link(dve.tensor_reduce(mx, dst, AX.X, ALU.max))
                own.link(dve.tensor_tensor(dst, dst, over(mx, n), ALU.is_equal))

            first_max(gsel, gsc, i_desc[:, NE - NG:NE], NG)
            gflat = gsel.rearrange("p t g -> p (t g)")
            own.link(dve.tensor_tensor(grp(rtv(2)), grp(rtv(1)), gflat.unsqueeze(2).to_broadcast([P, T * NG, EG]), ALU.mult))
            own.link(dve.tensor_scalar(gsel, gsel, 1.0, -NEG, ALU.subtract, ALU.mult))
            own.link(dve.tensor_tensor(grp(rtv(2)), grp(rtv(2)), gflat.unsqueeze(2).to_broadcast([P, T * NG, EG]), ALU.add))
            first_max(rtv(3), rtv(2), i_desc, NE)
            own.link(dve.scalar_tensor_tensor(rtv(2), rtv(3), -3.0e38, rtv(2), ALU.mult, ALU.add))
            first_max(rtv(4), rtv(2), i_desc, NE)
            dve.tensor_tensor(disp, rtv(3), rtv(4), ALU.add).then_inc(dispatch_ready, 1)
            for i in range(2):
                own.link(dve.tensor_tensor(rtv(2), rtv(3 + i), rtv(0), ALU.mult))
                own.link(dve.tensor_reduce(gatew[:, i, :], rtv(2), AX.X, ALU.add))
            own.link(dve.tensor_tensor(mx, gatew[:, 0, :], gatew[:, 1, :], ALU.add))
            own.link(dve.reciprocal(mx, mx))
            own.link(dve.tensor_tensor(gatew, gatew, mx.unsqueeze(1).to_broadcast([P, 2, T]), ALU.mult))
            dve.wait_ge(rank_ps, 1)
            own.link(dve.tensor_copy(cnt[:, 0, :], bank(1)[:, 0:NE]))
            own.link(dve.tensor_tensor(more_than, cnt[:, 0:1, :].rearrange("p a e -> p (a e)").unsqueeze(2).to_broadcast([P, NE, T - 1]),
                                       i_thr.unsqueeze(1).to_broadcast([P, NE, T - 1]), ALU.is_gt))
            own.link(dve.tensor_reduce(cnt[:, 1, :], more_than, AX.X, ALU.add))
            own.link(dve.tensor_tensor(packing, cnt[0:1, 1, :].rearrange("p (a e) -> p a e", a=2), place[0:1].unsqueeze(1).to_broadcast([1, 2, NE // 2]), ALU.mult))
            own.link(dve.tensor_reduce(packed_sum, packing, AX.X, ALU.add))
            dve.tensor_copy(ntiles[0:1, 0:2], packed_sum)
            own.link(dve.tensor_scalar(cnt[:, 2, :], cnt[:, 1, :], 1.0, float(P), ALU.add, ALU.mult))
            dve.memset(cnt[:, 4, :], 0.0)
            own.link(dve.memset(hot_lo[:, 0, :], 0.0))
            own.link(dve.tensor_tensor_scan(cnt[:, 3, :], cnt[:, 2, :], cnt[:, 4, :], 0.0, ALU.add, ALU.add))
            dve.tensor_scalar(ntiles[0:1, 2:3], cnt[0:1, 3, NE - 1:NE], 1.0 / P, None, ALU.mult)
            own.link(dve.tensor_tensor(cnt[:, 4, :], cnt[:, 3, :], cnt[:, 2, :], ALU.subtract))
            own.link(dve.tensor_tensor(rtv(1), bank(0)[:, 0:T * NE].rearrange("p (t e) -> p t e", t=T),
                                       cnt[:, 4:5, :].to_broadcast([P, T, NE]), ALU.add))
            for i in range(2):
                own.link(dve.tensor_tensor(rtv(2), rtv(3 + i), rtv(1), ALU.mult))
                own.link(dve.tensor_reduce(slot[:, i, :], rtv(2), AX.X, ALU.add))
            own.link(dve.tensor_copy(sloti[:, :, :], slot))
            own.link(dve.tensor_scalar(parts[:, 0], sloti[:, :, :], P - 1, None, ALU.bitwise_and))
            own.link(dve.tensor_scalar(parts[:, 1], sloti[:, :, :], 7, None, ALU.logical_shift_right))
            own.link(dve.tensor_copy(partf, parts[:, :, :, :]))
            dve.tensor_tensor(hot_lo, i_lo.unsqueeze(1).to_broadcast([P, 2 * T, P]),
                              partf[:, 0].rearrange("p a t -> p (a t)").unsqueeze(2).to_broadcast([P, 2 * T, P]), ALU.is_equal)
            own.link(dve.tensor_tensor(hot_tile, i_lo[:, 0:32].unsqueeze(1).to_broadcast([P, 2 * T, 32]),
                                       partf[:, 1].rearrange("p a t -> p (a t)").unsqueeze(2).to_broadcast([P, 2 * T, 32]), ALU.is_equal))
            dve.tensor_scalar(hot_hi[:, :, 0:32], hot_tile, i_tok[:, 0:1], None, ALU.mult)
            for i in range(2):
                last = dve.tensor_tensor(hot_hi[:, i * T:(i + 1) * T, 32:64], hot_tile[:, i * T:(i + 1) * T, :], over(i_lo[:, 0:T], 32), ALU.mult)
            last.then_inc(hot_ready, 1)
            dve.wait_ge(tok_ps, 1)
            own.link(dve.tensor_copy(tok_sum, bank(2)[:, 0:64]))
            dve.scalar_tensor_tensor(tok[:, :], tok_sum[:, 32:64], float(P), tok_sum[:, 0:32], ALU.mult, ALU.add).then_inc(tok_ready, 1)

            def split_lo(e, u):
                dve.wait_ge(xw_hi, e * UNITS + u + 1)
                dve.tensor_tensor(unit_split(u, 1), unit_slot(u), unit_split(u, 0).bitcast(F32), ALU.subtract).then_inc(xw_lo, 1)

            def rows_lo(j):
                dve.wait_ge(xe_hi, j + 1)
                dve.tensor_tensor(XR[:, 1], psum[:, 4:6, :].rearrange("p a (k n) -> p (a k) n", n=P), XR[:, 0].bitcast(F32),
                                  ALU.subtract).then_inc(xe_lo, 1)

            for u in range(6):
                split_lo(0, u)
            rows_lo(0)
            for u in range(6, UNITS):
                split_lo(0, u)

            def hidden(g, a):
                half = slice(a * DH2, (a + 1) * DH2)
                dve.wait_ge(up_ps, 2 * g + a + 1)
                dve.wait_ge(sil_sb, g + 1)
                dve.tensor_tensor(hid[:, half], sil[:, half], bank(up_bank[a])[:, 0:DH2], ALU.mult).then_inc(hid_sb, 1)

            def hidden_lo(g, a):
                dve.wait_ge(hr_hi, 2 * g + a + 1)
                dve.tensor_tensor(HR[:, 1, 2 * a:2 * a + 2], bank(hidT_bank[a])[:, 0:DH2].rearrange("p (f n) -> p f n", f=2),
                                  HR[:, 0, 2 * a:2 * a + 2].bitcast(F32), ALU.subtract).then_inc(hr_lo, 1)

            def body(e, g, last_tile, more):
                def split(*units):
                    if last_tile and more:
                        for u in units:
                            split_lo(e + 1, u)

                split(0)
                hidden(g, 0)
                split(1, 2)
                hidden_lo(g, 0)
                hidden(g, 1)
                split(3)
                hidden_lo(g, 1)
                rows_lo(g + 1)
                split(4, 5, 6, 7, 8, 9, 10, 11)

            each_tile(dve, "dve", body, own)
            def gated(t, i):
                xr = final(t, 2)
                return dve.scalar_tensor_tensor(xr, final(t, i), gatew[:, i, t:t + 1], xr, ALU.mult, ALU.add)

            for t in range(T + 1):
                if t < T:
                    dve.wait_ge(x1_scaled, t + 1)
                    dve.wait_ge(y_in[t % SETS], 32 * (t // SETS + 1))
                    first = own.done(gated(t, 0))
                if t > 0:
                    r = rs_f[:, t - 1:t]
                    dve.wait_ge(fin_std, t)
                    own.link(dve.reciprocal(r, r))
                    dve.scalar_tensor_tensor(shift_f[:, t - 1:t], mv_f[:, t - 1, 0:1], -1.0, r, ALU.mult, ALU.mult).then_inc(fin_rstd, 1)
                if t < T:
                    dve.wait_ge(dve_own, first)
                    own.link(gated(t, 1))
                    for i in range(2):
                        last = dve.bn_stats(st_c[:, i, :], final(t, 2)[:, i * 512:(i + 1) * 512])
                    wait_apart(dve, dve_own, own.done(last))
                    dve.bn_aggr(mv_f[:, t, :], st_c).then_inc(fin_stats, 1)
                if t == 1:
                    dve.wait_ge(ln2_in, 32)
                if t > 0:
                    dve.wait_ge(fin_norm, t)
                    dve.tensor_tensor(final(t - 1, 0), final(t - 1, 1), ln2[:, 0, :], ALU.mult).then_inc(scaled_ready, 1)

        @block.sync
        def _(sp):
            for t in range(T):
                sp.dma_start(stage[:, t, :], x_tiles[t]).then_inc(st_full[t], 16)
            n = 0
            for c0, width in GROUPS:
                for u in range(4):
                    if n < 8:
                        sp.wait_ge(xt_ready, n + 1)
                    else:
                        sp.wait_ge(w_lo, n - 8 + 1)
                    sp.dma_start(staged_unit(n)[:, 0:2 * width].rearrange("p (k n) -> p k n", k=2),
                                 win_v[:, 2 * u:2 * u + 2, c0:c0 + width]).then_inc(st_full[n % 8], 16)
                    n += 1
            for k in range(KC):
                sp.wait_ge(w_lo, n - 8 + 1)
                sp.dma_start(staged_unit(n), wout_v[k]).then_inc(st_full[n % 8], 16)
                n += 1
            def load_kqv(ch):
                c, b = ch.c, ch.b
                rng = bass.ds(c * P, P)
                sp.dma_start(kin[b], k_dram[rng, :].rearrange("p (h n) -> p h n", h=HEADS)).then_inc(kq_in[b], 16)
                sp.dma_start(qin[b], q_dram[:, :, rng]).then_inc(kq_in[b], 16)
                sp.dma_start(vau[b][:, :, 0:DH], v_dram[rng, :].rearrange("p (h n) -> p h n", h=HEADS)).then_inc(v_in[b], 16)

            def load_nm(ch):
                sp.dma_start(nm[ch.b], nm_dram[bass.ds(ch.c * HEADS, HEADS), :].partition_broadcast(P)).then_inc(nm_in[ch.b], 16)

            def load_og_hb(ch):
                b, rng = ch.b, bass.ds(ch.c * P, P)
                sp.dma_start(hbin[b], hb_dram[rng, :]).then_inc(og_hb_in[b], 16)
                sp.dma_start(og[b], og_dram[rng, :].rearrange("p (h n) -> p h n", h=HEADS)).then_inc(og_hb_in[b], 16)

            def load_x(ch):
                sp.dma_start(xin[ch.b], x[0][bass.ds(ch.c * P, P), :]).then_inc(x_in[ch.b], 16)

            def store_x1(ch):
                sp.wait_ge(x1_ready, ch.c + 1)
                sp.dma_start(x1_dram[bass.ds(ch.c * P, P), :], x1s).then_inc(x1_out, 16)

            def step(ch):
                if 1 <= ch.n < T - 1:
                    sp.wait_ge(hT_ps, ch.c)
                if ch.n == 0:
                    sp.wait_ge(w_lo, 28 + 4)
                if ch.n < T - 1:
                    load_kqv(ch.plus(1))
                    load_nm(ch.plus(1))
                    load_og_hb(ch.plus(1))
                if ch.n >= 2:
                    store_x1(ch.plus(-2))
                if ch.n < T:
                    load_x(ch)

            first = Chunk(0, 0, 0)
            sp.wait_ge(hb_out, 16)
            for i in range(4):
                sp.wait_ge(ev_out[i], 16 * 6)
            load_kqv(first)
            sp.wait_ge(nm_out, 16)
            load_nm(first)
            for i in range(4):
                sp.wait_ge(ev_out[i], 16 * 8)
            load_og_hb(first)
            for i, v in enumerate((ln1_w, ln1_b)):
                sp.dma_start(ln1[:, i, :], v[0].partition_broadcast(P)).then_inc(ln1_in, 16)
            sp.dma_start(rw, router_w.rearrange("(p k) e -> p k e", k=KC)).then_inc(ln1_in, 16)
            chunk_steps(sp, step)
            sp_experts(sp)

        @block.gpsimd
        def _(pool):
            own = Links(pool, sem("pool_own"), "pool_links")
            for s in (lg_read, x1_out, x1T_ps, lg_ps, y_sb, y_out):
                pool.sem_inc(s, PRIMED)
            pool.memset(ones[:, :], 1.0)
            own.link(pool.memset(ident[:, :], 0.0))
            pool.affine_select(out=ident[:, :], in_=ident[:, :], compare_op=ALU.not_equal, fill=1.0, base=0,
                               pattern=[[-1, P]], channel_multiplier=1).then_inc(made, 1)
            pool.affine_select(out=tri[:, :], in_=ones[:, :], compare_op=ALU.is_ge, fill=0.0, base=0,
                               pattern=[[1, P]], channel_multiplier=-1).then_inc(made, 1)
            for i in range(NE // 2):
                pool.memset(place[:, i:i + 1], float(T ** i))
            pool.iota(i_lo, pattern=[[1, P]], base=0, channel_multiplier=0, allow_small_or_imprecise_dtypes=True)
            pool.iota(i_desc, pattern=[[-1, NE]], base=NE, channel_multiplier=0, allow_small_or_imprecise_dtypes=True)
            pool.iota(i_thr, pattern=[[P, T - 1]], base=P, channel_multiplier=0, allow_small_or_imprecise_dtypes=True)
            own.link(pool.iota(i_tok, pattern=[[P, T]], base=0, channel_multiplier=1, allow_small_or_imprecise_dtypes=True))
            for dst, src in small_loads:
                pool.dma_start(dst, src).then_inc(small_in, 16)
            pool.wait_ge(small_in, 16 * SMALL_LOADS)
            pool.affine_select(out=wsl, in_=wsl, compare_op=ALU.is_ge, fill=0.0, base=0,
                               pattern=[[0, HEADS], [-1, P]], channel_multiplier=1).then_inc(made, 1)
            def weigh(ch):
                b = ch.b
                pool.wait_ge(nm_in[b], 16 * ch.r + 16)
                pool.tensor_tensor(nm[b], nm[b], nmask.unsqueeze(1).to_broadcast([P, HEADS, P]), ALU.add).then_inc(nm_masked, 1)
                pool.wait_ge(v_in[b], 16 * ch.r + 16)
                pool.wait_ge(ones_col, 1)
                if ch.n:
                    pool.wait_ge(state_ps, ch.c)
                pool.tensor_tensor(vw, vau[b], w4[:, 0, bass.ds(ch.c * HEADS, HEADS)].unsqueeze(2).to_broadcast([P, HEADS, DH + 1]),
                                   ALU.mult).then_inc(vw_sb, 1)

            s = 0
            for g in range(3, 7):
                for j in range(JOBS):
                    if g < 6:
                        pool.wait_ge(proj_read, g * JOBS + j + 1)
                    else:
                        pool.wait_ge(og_ready, j + 1)
                    if g == 3:
                        dst = q_dram[:, j // 2, (j % 2) * 512:(j % 2) * 512 + 512]
                    else:
                        dst = (k_dram, v_dram, og_dram)[g - 4][j * P:(j + 1) * P, :]
                    pool.dma_start(dst, ev[:, s % 4, :]).then_inc(ev_out[s % 4], 16)
                    s += 1
                    if g == 6 and j == 2:
                        pool.wait_ge(g_nm, 1)
                        pool.dma_start(nm_dram, gT[0:NC_, 2, :]).then_inc(nm_out, 16)
                    if g == 6 and j == 4:
                        pool.wait_ge(g_wk, 1)
                        weigh(Chunk(0, 0, 0))
                if g == 5:
                    pool.wait_ge(hb_ready, 4)
                    pool.dma_start(hb_dram.rearrange("(t p) n -> p t n", p=P), ug).then_inc(hb_out, 16)
                    own.link(pool.memset(nmask, 0.0))
                    own.link(pool.affine_select(out=nmask, in_=nmask, compare_op=ALU.is_ge, fill=NEG, base=0,
                                                pattern=[[1, P]], channel_multiplier=-1))
                    pool.wait_ge(hb_out, 16)
                    pool.memset(vau[0][:, :, DH:DH + 1], 1.0).then_inc(ones_col, 1)
            def step(ch):
                if ch.n < T - 1:
                    weigh(ch.plus(1))

            pool.wait_ge(w_lo, 28 + 4)
            pool.memset(vau[1][:, :, DH:DH + 1], 1.0).then_inc(ones_col, 1)
            pool.wait_ge(ones_col, 2)
            chunk_steps(pool, step)
            pool_experts(pool, own)

        @block.tensor
        def _(pe):
            pe.wait_ge(made, 2)
            for t in range(T):
                pe.wait_ge(st_full[t], 16)
                if t >= 2:
                    pe.wait_ge(xt_lo, t - 1)
                b = 4 + 2 * (t % 2)
                for k in range(KC):
                    last = pe.transpose(psum[:, b + k // 4, (k % 4) * P:(k % 4 + 1) * P], stage[:, t, k:D:KC], ident[:, :])
                last.then_inc(xt_ready, 1)
            pe.wait_ge(made, 3)
            pe.wait_ge(xt_lo, T)
            for h in range(HEADS):
                pe.transpose(bank(4)[:, h * P:(h + 1) * P], wsl[:, h, :], ident[:, :])
            pe.wait_ge(small_in, 16 * SMALL_LOADS)
            pe.transpose(bank(5)[:, 0:80], packed, ident[0:80, 0:80]).then_inc(ws_ready, 1)

            def group(g, width, features, turn=0, first=False, jobs=range(JOBS)):
                for j in jobs:
                    if not (first and j < 4):
                        pe.wait_ge(proj_read, g * JOBS + j - 3)
                    b = bank(j % 4)
                    for k in range(KC):
                        if j == 0 and k % 2 == 0:
                            pe.wait_ge(w_lo, g * 4 + k // 2 + 1)
                        for i, (hx, hw) in enumerate(((0, 0), (1, 0), (0, 1))):
                            if features:
                                f, half = (j // 2 + turn) % 4, j % 2
                                last = pe.matmul(b, wc[:, hw, k, f * P:(f + 1) * P], xT[:, hx, k, half * 512:half * 512 + 512],
                                                 start=(k == 0 and i == 0), stop=(k == KC - 1 and i == 2))
                            else:
                                last = pe.matmul(b[:, 0:width], xT[:, hx, k, j * P:(j + 1) * P], wc[:, hw, k, 0:width],
                                                 start=(k == 0 and i == 0), stop=(k == KC - 1 and i == 2))
                        if j == JOBS - 1 and k % 2 == 1 and k < KC - 1:
                            last.then_inc(w_free, 1)
                    last.then_inc(proj_done, 1)

            group(0, GROUPS[0][1], False, first=True)
            group(1, GROUPS[1][1], False)
            pe.wait_ge(g_logf, 1)
            pe.matmul(bank(5)[:, 0:NC_], tri[:, :], gt[:, 2, :], start=True, stop=True)
            pe.matmul(bank(5)[:, NC_:2 * NC_], ones[:, :], gt[:, 2, :], start=True, stop=True).then_inc(g_sums, 1)
            group(2, GROUPS[2][1], True, turn=2)
            pe.wait_ge(g_u, 1)
            pe.transpose(bank(5)[0:NC_, 128:256], uS, ident[:, :])
            pe.transpose(bank(5)[0:NC_, 256:384], gt[:, 6, :], ident[:, :]).then_inc(g_uT, 1)
            group(3, GROUPS[3][1], True)
            pe.wait_ge(g_cm, 1)
            pe.transpose(bank(5)[:, 384:384 + NC_], gT[0:NC_, 0, :], ident[0:NC_, 0:NC_])
            pe.transpose(bank(5)[0:1, 448:448 + NC_], gT[0:NC_, 1, 0:1], ident[0:NC_, 0:NC_]).then_inc(g_back, 1)
            pe.wait_ge(z_ready, 1)
            pe.wait_ge(ws_read, 1)
            for h in range(HEADS - 1):
                pe.matmul(bank((4, 6, 7)[h]), wsT[:, h, :], gvs[:, :, h * GHD:(h + 1) * GHD], start=True, stop=True).then_inc(z_mixed, 1)
            group(4, GROUPS[4][1], False)
            pe.wait_ge(hb_ready, 1)
            pe.matmul(bank(4), wsT[:, HEADS - 1, :], gvs[:, :, (HEADS - 1) * GHD:HEADS * GHD], start=True, stop=True).then_inc(z_mixed, 1)
            pe.wait_ge(g_m, 1)
            pe.matmul(bank(5)[:, 64:64 + 2 * NC_], ones[0:1, :], grow[0:1, 1:3, :], start=True, stop=True).then_inc(g_bc, 1)
            group(5, GROUPS[5][1], False)
            group(6, GROUPS[6][1], False, jobs=range(0, 1))
            pe.wait_ge(g_w, 1)
            pe.transpose(bank(5)[0:NC_, 0:P], gt[:, 0, :], ident[:, :]).then_inc(g_nmT, 1)

            def channel_sums(src, signal):
                for half in range(2):
                    for f in range(2):
                        last = pe.matmul(bank(6 + half), ones[:, :], src[:, f, half * 512:half * 512 + 512], start=(f == 0), stop=(f == 1))
                last.then_inc(signal, 1)

            group(6, GROUPS[6][1], False, jobs=range(1, 2))
            pe.wait_ge(taps_done, 1)
            pe.wait_ge(hb_ready, 4)
            channel_sums(acc, cv_sum)
            group(6, GROUPS[6][1], False, jobs=range(2, 5))
            pe.wait_ge(cv_sq, 1)
            channel_sums(gvs.rearrange("p t n -> p (t n)").rearrange("p (f n) -> p f n", f=2), cv_var)
            group(6, GROUPS[6][1], False, jobs=range(5, JOBS))

            def transpose_k(ch):
                pe.wait_ge(kq_in[ch.b], 32 * ch.r + 32)
                if ch.n >= 2:
                    pe.wait_ge(xr_lo, ch.c - 1)
                for h in range(HEADS):
                    last = pe.transpose(bank(0)[:, h * P:(h + 1) * P], kin[ch.b][:, h, :], ident[:, :])
                last.then_inc(kT_ps, 1)

            def scores(ch):
                pe.wait_ge(kq_in[ch.b], 32 * ch.r + 32)
                pe.wait_ge(kT_sb, ch.c + 1)
                for h in range(HEADS):
                    last = pe.matmul(bank(1)[:, h * P:(h + 1) * P], kT[:, h, :], qin[ch.b][:, h, :], start=True, stop=True)
                last.then_inc(st_ps, 1)

            def numerators(ch):
                c, b = ch.c, ch.b
                pe.wait_ge(v_in[b], 16 * ch.r + 16)
                pe.wait_ge(ones_col, 1 if ch.n == 0 else 2)
                pe.wait_ge(pt_sb, c + 1)
                pe.wait_ge(c_sb, c + 1)
                if ch.n >= 3:
                    pe.wait_ge(lg_read, PRIMED + c - 2)
                elif ch.n >= 1:
                    pe.wait_ge(num_sb, c)
                    pe.wait_ge(lg_read, PRIMED + c - 2)
                for h in range(HEADS):
                    o = (h % 2) * (DH + 1)
                    pe.matmul(psum[:, 4 + h // 2, o:o + DH + 1], qin[b][:, h, :], C[:, h, :], start=True, stop=True)
                for h in range(HEADS):
                    o = (h % 2) * (DH + 1)
                    last = pe.matmul(psum[:, 2 + h // 2, o:o + DH + 1], nm[b][:, h, :], vau[b][:, h, :], start=True, stop=True)
                last.then_inc(ii_ps, 1)

            def state_products(ch):
                pe.wait_ge(vw_sb, ch.c + 1)
                pe.wait_ge(inter_sb, ch.c + 1)
                for h in range(HEADS):
                    o = (h % 2) * (DH + 1)
                    last = pe.matmul(psum[:, 4 + h // 2, o:o + DH + 1], kin[ch.b][:, h, :], vw[:, h, :], start=True, stop=True)
                last.then_inc(state_ps, 1)

            def out_projection(ch, half, ks):
                if half == 0:
                    pe.wait_ge(xr_lo, ch.c + 1)
                if ks[0] == 0 and ch.n >= 1:
                    pe.wait_ge(y_summed, 2 * ch.c - 1 + half)
                for k in ks:
                    for i, (hx, hw) in enumerate(((0, 0), (1, 0), (0, 1))):
                        last = pe.matmul(bank(6 + half), XRb[ch.b][:, hx, k, :], wo[:, hw, k, half * 512:half * 512 + 512],
                                         start=(k == 0 and i == 0), stop=(k == KC - 1 and i == 2))
                if ks[-1] == KC - 1:
                    last.then_inc(y_half, 1)

            def transpose_x1(ch):
                pe.wait_ge(ln1_in, 48)
                pe.wait_ge(x1_ready, ch.c + 1)
                if ch.n < T - 2:
                    pe.wait_ge(num_sb, ch.c + 3)
                else:
                    pe.wait_ge(num_sb, T)
                    pe.wait_ge(lg_read, PRIMED + ch.c)
                for k in range(KC):
                    last = pe.transpose(psum[:, 2 + k // 4, (k % 4) * P:(k % 4 + 1) * P], x1s[:, k:D:KC], ident[:, :])
                last.then_inc(x1T_ps, 1)

            def route(ch):
                pe.wait_ge(x1T_sb, ch.c + 1)
                for k in range(KC):
                    last = pe.matmul(bank(2)[:, 0:NE], x1T[:, k * P:(k + 1) * P], rw[:, k, :], start=(k == 0), stop=(k == KC - 1))
                last.then_inc(lg_ps, 1)

            def transpose_h(ch):
                pe.wait_ge(ha_ready, ch.c + 1)
                pe.wait_ge(og_hb_in[ch.b], 32 * ch.r + 32)
                if ch.n < T - 1:
                    pe.wait_ge(kT_sb, ch.c + 2)
                    pe.wait_ge(pt_sb, ch.c + 2)
                for h in range(HEADS):
                    pe.transpose(bank(0)[:, h * P:(h + 1) * P], ha[:, h, :], ident[:, :])
                for k in range(2):
                    last = pe.transpose(bank(1)[:, k * P:(k + 1) * P], hbin[ch.b][:, k * P:(k + 1) * P], ident[:, :])
                last.then_inc(hT_ps, 1)

            def step(ch):
                n = ch.n
                mixes, projects, routes = n < T, 1 <= n <= T, n >= 2
                if mixes:
                    numerators(ch)
                if projects:
                    if n == 1:
                        pe.wait_ge(w_lo, 28 + KC)
                    out_projection(ch.plus(-1), 0, range(KC))
                if mixes:
                    state_products(ch)
                if n < T - 1:
                    transpose_k(ch.plus(1))
                if projects:
                    out_projection(ch.plus(-1), 1, range(KC // 2))
                if n < T - 1:
                    scores(ch.plus(1))
                if routes:
                    transpose_x1(ch.plus(-2))
                if mixes:
                    transpose_h(ch)
                if projects:
                    out_projection(ch.plus(-1), 1, range(KC // 2, KC))
                if routes:
                    route(ch.plus(-2))

            pe.wait_ge(proj_read, 7 * JOBS)
            transpose_k(Chunk(0, 0, 0))
            scores(Chunk(0, 0, 0))
            chunk_steps(pe, step)
            pe_experts(pe)

        @block.scalar
        def _(act):
            own = Links(act, act_own, "act_links")
            for t in range(T):
                act.wait_ge(xt_ready, t + 1)
                b = 4 + 2 * (t % 2)
                act.activation(xT[:, 0, :, t * P:(t + 1) * P], psum[:, b:b + 2, :].rearrange("p a (k n) -> p (a k) n", n=P),
                               AF.Copy).then_inc(xt_hi, 1)

            def split_hi(g, u):
                n, width = 4 * g + u, GROUPS[g][1]
                act.wait_ge(st_full[n % 8], 16 * (n // 8 + 2))
                if g and u < 3:
                    act.wait_ge(w_free, 3 * (g - 1) + u + 1)
                elif g:
                    act.wait_ge(proj_done, JOBS * g)
                act.activation(wc[:, 0, 2 * u:2 * u + 2, 0:width],
                               staged_unit(n)[:, 0:2 * width].rearrange("p (k n) -> p k n", k=2), AF.Copy).then_inc(w_hi, 1)

            for u in range(4):
                split_hi(0, u)
            for g in range(2):
                for t in range(T):
                    if t == T - 1:
                        for u in range(4):
                            split_hi(g + 1, u)
                    act.wait_ge(proj_read, g * JOBS + t + 1)
                    act.activation((ug, gvs)[g][:, t, :], ev[:, t % 2, 0:GW], AF.Gelu_apprx_tanh).then_inc(act_done, 1)
                if g == 0:
                    own.link(act.activation(gt[:, 0, :].rearrange("p (t h) -> p t h", t=T), gates[:, :, HEADS:2 * HEADS], AF.Abs))
                    own.link(act.activation(gt[:, 0, :], gt[:, 0, :], AF.Exp, scale=-1.0))
                    act.activation(gt[:, 1, :], gt[:, 0, :], AF.Ln, bias=1.0).then_inc(g_ln, 1)
            for j in range(4):
                act.wait_ge(proj_read, 2 * JOBS + j + 1)
                v = acc[:, j // 2, (j % 2) * 512:(j % 2) * 512 + 512]
                act.activation(v, v, AF.Sigmoid).then_inc(act_done, 1)
            act.wait_ge(gv_stats, 1)
            own.link(act.activation(rs_a, mv_a[:, :, 1], AF.Ln, bias=LN_EPS))
            act.activation(rs_a, rs_a, AF.Exp, scale=-0.5).then_inc(gv_rstd, 1)
            for u in range(4):
                split_hi(3, u)
            for g in range(4, 7):
                for u in range(4):
                    split_hi(g, u)
            act.wait_ge(g_w, 1)
            act.activation(w4, w4, AF.Exp).then_inc(g_we, 1)
            def output_gate(j):
                act.wait_ge(proj_read, 6 * JOBS + j + 1)
                act.activation(ev[:, j % 4, :], ev[:, j % 4, :], AF.Sigmoid).then_inc(act_done, 1)

            output_gate(0)
            act.wait_ge(g_nmT, 1)
            act.activation(gT[0:NC_, 2, :], bank(5)[0:NC_, 0:P], AF.Copy).then_inc(g_nm, 1)
            for j in range(1, 4):
                output_gate(j)
                if j == 2:
                    cv = gvs.rearrange("p t n -> p (t n)").rearrange("p (f n) -> p f n", f=2)
                    act.wait_ge(cv_mid, 1)
                    act.activation(cv, acc, AF.Square).then_inc(cv_sq, 1)
            output_gate(4)
            act.wait_ge(cv_var, 1)
            own.link(act.activation(cv[:, 0, :], psum[:, 6:8, :].rearrange("p a n -> p (a n)"), AF.Ln, scale=1.0 / CW, bias=LN_EPS))
            act.activation(cv[:, 0, :], cv[:, 0, :], AF.Exp, scale=-0.5).then_inc(cv_rstd, 1)
            def split_wout(ks):
                for k in ks:
                    n = 28 + k
                    act.wait_ge(st_full[n % 8], 16 * (n // 8 + 2))
                    act.wait_ge(proj_done, JOBS * 7)
                    act.activation(wo[:, 0, k, :], staged_unit(n), AF.Copy).then_inc(w_hi, 1)

            def copy_kT(ch):
                act.wait_ge(kT_ps, ch.c + 1)
                act.activation(kT, bank(0).rearrange("p (h n) -> p h n", h=HEADS), AF.Copy).then_inc(kT_sb, 1)

            def decays(ch):
                act.wait_ge(nm_masked, ch.c + 1)
                for h in range(HEADS):
                    v = nm[ch.b][:, h, :]
                    last = act.activation(v, v, AF.Exp, bias=uS[:, bass.ds(ch.c * HEADS + h, 1)])
                last.then_inc(e_sb, 1)

            def scale_inter(ch):
                act.wait_ge(ii_ps, ch.c + 1)
                if ch.n:
                    act.wait_ge(h_stats, ch.c)
                for h in range(HEADS):
                    o = (h % 2) * (DH + 1)
                    last = act.activation(num[:, h, :], psum[:, 4 + h // 2, o:o + DH + 1], AF.Copy,
                                          scale=w4[:, 2, bass.ds(ch.c * HEADS + h, 1)])
                last.then_inc(inter_sb, 1)

            def deviation(dst, var, eps, stats, count, signal):
                act.wait_ge(stats, count)
                act.activation(dst, var, AF.Sqrt, bias=eps).then_inc(signal, 1)

            def copy_x1T(ch):
                act.wait_ge(x1T_ps, PRIMED + ch.c + 1)
                act.wait_ge(lg_ps, PRIMED + ch.c)
                act.activation(x1T, psum[:, 2:4, :].rearrange("p a n -> p (a n)"), AF.Copy).then_inc(x1T_sb, 1)

            def split_h(ch):
                hi = XRb[ch.b][:, 0]
                act.wait_ge(hT_ps, ch.c + 1)
                if ch.n >= 2:
                    act.wait_ge(y_half, 2 * ch.c - 2)
                act.activation(hi[:, 0:4, :], bank(0).rearrange("p (h n) -> p h n", h=HEADS), AF.Copy)
                act.activation(hi[:, 4:6, :], bank(1)[:, 0:256].rearrange("p (h n) -> p h n", h=2), AF.Copy)
                act.activation(hi[:, 6:8, :], acc[:, :, bass.ds(ch.c * P, P)], AF.Copy).then_inc(xr_hi, 1)

            def step(ch):
                n = ch.n
                if n >= 2:
                    deviation(rs_c, mv_c[:, 1:2], LN_EPS, r_stats, ch.c - 1, r_std)
                if n < T:
                    scale_inter(ch)
                    if n == 0:
                        split_wout(range(4, 6))
                    deviation(rs_b, mv_b[:, :, 1], ML_EPS, h_stats, ch.c + 1, h_std)
                if n == 0:
                    split_wout(range(6, KC))
                if n < T - 1:
                    copy_kT(ch.plus(1))
                    decays(ch.plus(1))
                if n >= 2:
                    copy_x1T(ch.plus(-2))
                if n < T:
                    split_h(ch)

            decays(Chunk(0, 0, 0))
            for j in range(5, JOBS):
                output_gate(j)
            copy_kT(Chunk(0, 0, 0))
            split_wout(range(4))
            act.wait_ge(cv_norm, 1)
            for f in range(2):
                last = act.activation(acc[:, f, :], acc[:, f, :], AF.Silu, scale=convc[:, 1, f:f + 1], bias=convc[:, 2, f:f + 1])
            last.then_inc(cv_done, 1)
            chunk_steps(act, step, own)
            act_experts(act, own)

        @block.vector
        def _(dve):
            own = Links(dve, dve_own, "dve_links")
            dve.memset(cpad[:, :, 0:TAPS - 1], 0.0)
            own.link(dve.memset(gT[:, 2, :], 0.0))
            for t in range(T):
                dve.wait_ge(xt_hi, t + 1)
                b = 4 + 2 * (t % 2)
                dve.tensor_tensor(xT[:, 1, :, t * P:(t + 1) * P], psum[:, b:b + 2, :].rearrange("p a (k n) -> p (a k) n", n=P),
                                  xT[:, 0, :, t * P:(t + 1) * P].bitcast(F32), ALU.subtract).then_inc(xt_lo, 1)

            def split_lo(g, u):
                n, width = 4 * g + u, GROUPS[g][1]
                dve.wait_ge(w_hi, n + 1)
                dve.tensor_tensor(wc[:, 1, 2 * u:2 * u + 2, 0:width],
                                  staged_unit(n)[:, 0:2 * width].rearrange("p (k n) -> p k n", k=2),
                                  wc[:, 0, 2 * u:2 * u + 2, 0:width].bitcast(F32), ALU.subtract).then_inc(w_lo, 1)

            for u in range(4):
                split_lo(0, u)
            dve.wait_ge(ws_ready, 1)
            own.link(dve.tensor_copy(cols, bank(5)[:, 0:80]))
            dve.tensor_copy(wsT, bank(4).rearrange("p (h n) -> p h n", h=HEADS)).then_inc(ws_read, 1)
            dve.wait_ge(small_in, 16 * SMALL_LOADS)

            f_pre, i_pre = gates[:, :, HEADS:2 * HEADS], gates[:, :, 0:HEADS]

            def tab(r):
                return gt[:, r, :].rearrange("p (t h) -> p t h", t=T)

            for g in range(2):
                for t in range(T):
                    if t == T - 1:
                        for u in range(4):
                            split_lo(g + 1, u)
                    n = g * JOBS + t
                    dve.wait_ge(proj_done, n + 1)
                    o = 0
                    if g == 0:
                        o = 2 * HEADS
                        dve.tensor_tensor(gates[:, t, :], bank(t % 4)[:, 0:o], b_tm[:, 0, 0:o], ALU.add)
                    if n >= 2:
                        dve.wait_ge(act_done, n - 1)
                    dve.tensor_tensor(ev[:, t % 2, 0:GW], bank(t % 4)[:, o:o + GW], b_tm[:, g, o:o + GW], ALU.add).then_inc(proj_read, 1)
                    if g == 1 and t == 3:
                        dve.wait_ge(g_ln, 1)
                        dve.scalar_tensor_tensor(tab(2), f_pre, 0.0, tab(1), ALU.min, ALU.subtract).then_inc(g_logf, 1)

            def gv_statistics():
                for t in range(T):
                    dve.wait_ge(act_done, T + t + 1)
                    own.link(dve.bn_stats(st_a[:, t, :], gvs[:, t, :]))
                    last = dve.bn_aggr(mv_a[:, t, :], st_a[:, t, :])
                last.then_inc(gv_stats, 1)

            def gate_sums():
                dve.wait_ge(g_sums, 1)
                dve.tensor_copy(gt[:, 3, :], bank(5)[:, 0:NC_])
                own.link(dve.tensor_copy(gt[:, 4, :], bank(5)[:, NC_:2 * NC_]))
                own.link(dve.tensor_tensor(uS.rearrange("p (t h) -> p t h", t=T), i_pre, tab(3), ALU.subtract))
                dve.tensor_tensor(gt[:, 6, :], gt[:, 4, :], uS, ALU.add).then_inc(g_u, 1)

            for j in range(JOBS):
                if j == JOBS - 1:
                    for u in range(4):
                        split_lo(3, u)
                n = 2 * JOBS + j
                f, half = (j // 2 + 2) % 4, j % 2
                dve.wait_ge(proj_done, n + 1)
                if f >= 2:
                    dve.tensor_scalar(acc[:, f - 2, half * 512:half * 512 + 512], bank(j % 4), bq_fm[:, 4 + f:5 + f], None,
                                      ALU.add).then_inc(proj_read, 1)
                else:
                    dve.wait_ge(act_done, 2 * T + 4)
                    dve.scalar_tensor_tensor(cpad[:, f, TAPS - 1 + half * 512:TAPS - 1 + half * 512 + 512], bank(j % 4),
                                             bq_fm[:, 4 + f:5 + f], acc[:, f, half * 512:half * 512 + 512],
                                             ALU.add, ALU.mult).then_inc(proj_read, 1)
                if j == 0:
                    gv_statistics()
                if j == 2:
                    gate_sums()

            def tap(i):
                for f in range(2):
                    if i == 0:
                        last = dve.tensor_scalar(acc[:, f, :], cpad[:, f, 0:SEQ], convw[:, f, 0:1], convc[:, 0, f:f + 1], ALU.mult, ALU.add)
                    else:
                        last = dve.scalar_tensor_tensor(acc[:, f, :], cpad[:, f, i:i + SEQ], convw[:, f, i:i + 1], acc[:, f, :],
                                                        ALU.mult, ALU.add)
                return own.done(last)

            dve.wait_ge(proj_read, 3 * JOBS)
            tapped = tap(0)

            def z_norm():
                dve.wait_ge(gv_rstd, 1)
                for t in range(T):
                    last = dve.tensor_scalar(gvs[:, t, :], gvs[:, t, :], mv_a[:, t, 0:1], rs_a[:, t:t + 1], ALU.subtract, ALU.mult)
                own.link(last)
                own.link(dve.tensor_tensor(gvs, gvs, gnw[:, 0:1, :].to_broadcast([P, T, GW]), ALU.mult))
                dve.tensor_tensor(gvs, gvs, gnw[:, 1:2, :].to_broadcast([P, T, GW]), ALU.add).then_inc(z_ready, 1)

            def cummax():
                dve.wait_ge(g_uT, 1)
                own.link(dve.tensor_tensor_scan(gT[0:NC_, 0, :], gT[0:NC_, 2, :], bank(5)[0:NC_, 128:256], -3.0e38, ALU.add, ALU.max))
                dve.tensor_reduce(gT[0:NC_, 1, 0:1], bank(5)[0:NC_, 256:384], AX.X, ALU.max).then_inc(g_cm, 1)

            def m_scan():
                dve.wait_ge(g_back, 1)
                dve.tensor_copy(gt[:, 7, :], bank(5)[:, 384:384 + NC_])
                dve.memset(grow[0:1, 2, 0:HEADS], 0.0)
                own.link(dve.tensor_copy(grow[0:1, 0, :], bank(5)[0:1, 448:448 + NC_]))
                for h in range(HEADS):
                    last = dve.tensor_tensor_scan(grow[0:1, 1, h:NC_:HEADS], gt[0:1, 4, h:NC_:HEADS], grow[0:1, 0, h:NC_:HEADS], 0.0,
                                                  ALU.add, ALU.max)
                own.link(last)
                dve.tensor_copy(grow[0:1, 2, HEADS:NC_], grow[0:1, 1, 0:NC_ - HEADS]).then_inc(g_m, 1)

            def mix_z(h):
                dve.wait_ge(z_mixed, h + 1)
                v = ug[:, :, h * GHD:(h + 1) * GHD]
                dve.scalar_tensor_tensor(v, bank((4, 6, 7, 4)[h]).rearrange("p (t n) -> p t n", t=T), bs_col[:, h:h + 1], v,
                                         ALU.add, ALU.mult).then_inc(hb_ready, 1)

            def gate_args():
                dve.wait_ge(g_bc, 1)
                own.link(dve.tensor_copy(gt[:, 8:10, :], bank(5)[:, 64:64 + 2 * NC_].rearrange("p (a n) -> p a n", a=2)))
                own.link(dve.tensor_tensor(gt[:, 7, :], gt[:, 9, :], gt[:, 7, :], ALU.max))
                dve.tensor_tensor(w4[:, 0, :], gt[:, 6, :], gt[:, 8, :], ALU.subtract)
                own.link(dve.tensor_tensor(gt[:, 5, :], gt[:, 4, :], gt[:, 9, :], ALU.add))
                dve.tensor_tensor(w4[:, 1, :], gt[:, 5, :], gt[:, 8, :], ALU.subtract)
                dve.tensor_tensor(w4[:, 2, :], gt[:, 9, :], gt[:, 7, :], ALU.subtract)
                dve.scalar_tensor_tensor(w4[:, 3, :], gt[:, 3, :], -1.0, gt[:, 7, :], ALU.mult, ALU.subtract)
                dve.tensor_scalar(gt[:, 0, :], gt[:, 7, :], -1.0, None, ALU.mult).then_inc(g_w, 1)

            def weigh_og(j):
                s = j % 4
                dve.wait_ge(act_done, 2 * T + 4 + j + 1)
                dve.tensor_tensor(ev[:, s, :], ev[:, s, :], mlw, ALU.mult).then_inc(og_ready, 1)

            cvr = gvs.rearrange("p t n -> p (t n)").rearrange("p (f n) -> p f n", f=2)
            s, taps = 0, 1
            for g in range(3, 7):
                for j in range(JOBS):
                    n = g * JOBS + j
                    if j == JOBS - 1 and g < 6:
                        for u in range(4):
                            split_lo(g + 1, u)
                    dve.wait_ge(proj_done, n + 1)
                    if s >= 4:
                        dve.wait_ge(ev_out[s % 4], 16 * (s // 4))
                    if g == 3:
                        dve.tensor_scalar(ev[:, s % 4, :], bank(j % 4), bq_fm[:, j // 2:j // 2 + 1], None, ALU.add).then_inc(proj_read, 1)
                    else:
                        dve.tensor_tensor(ev[:, s % 4, :], bank(j % 4), b_tm[:, g - 2, :], ALU.add).then_inc(proj_read, 1)
                    s += 1
                    for _ in range(2 if j % 2 else 1):
                        if taps < TAPS:
                            dve.wait_ge(dve_own, tapped)
                            tapped = tap(taps)
                            taps += 1
                            if taps == TAPS:
                                dve.wait_ge(dve_own, tapped)
                                dve.sem_inc(taps_done, 1)
                    if g == 3 and j == 0:
                        z_norm()
                    if g == 3 and j == 3:
                        cummax()
                    if g == 4 and j < 3:
                        mix_z(j)
                    if g == 4 and j == 3:
                        m_scan()
                    if g == 5 and j == 0:
                        mix_z(3)
                    if g == 5 and j == 1:
                        gate_args()
                    if g == 6 and j == 3:
                        dve.wait_ge(g_we, 1)
                        dve.tensor_scalar(w4[:, 0, :], w4[:, 0, :], KSCALE, None, ALU.mult).then_inc(g_wk, 1)
                    if g == 6 and j >= 1:
                        weigh_og(j - 1)
                    if g == 6 and j == 2:
                        dve.wait_ge(cv_sum, 1)
                        for f in range(2):
                            last = dve.scalar_tensor_tensor(acc[:, f, :], psum[:, 6:8, :].rearrange("p a n -> p (a n)"), -1.0 / CW,
                                                            acc[:, f, :], ALU.mult, ALU.add)
                        last.then_inc(cv_mid, 1)
                    if g == 6 and j == 6:
                        dve.wait_ge(cv_rstd, 1)
                        for f in range(2):
                            last = dve.tensor_tensor(acc[:, f, :], acc[:, f, :], cvr[:, 0, :], ALU.mult)
                        last.then_inc(cv_norm, 1)
            weigh_og(JOBS - 1)

            dve.memset(C, 0.0).then_inc(c_sb, 1)

            def split_wout(ks):
                for k in ks:
                    dve.wait_ge(w_hi, 28 + k + 1)
                    dve.tensor_tensor(wo[:, 1, k, :], staged_unit(28 + k), wo[:, 0, k, :].bitcast(F32), ALU.subtract).then_inc(w_lo, 1)

            def weigh_scores(ch):
                v = nm[ch.b]
                dve.wait_ge(e_sb, ch.c + 1)
                dve.wait_ge(st_ps, ch.c + 1)
                dve.scalar_tensor_tensor(v, bank(1).rearrange("p (h n) -> p h n", h=HEADS), KSCALE, v, ALU.mult, ALU.mult).then_inc(pt_sb, 1)

            def residual1(ch, half):
                v = xin[ch.b][:, half * 512:half * 512 + 512]
                dve.wait_ge(x_in[ch.b], 16 * ch.r + 16)
                dve.wait_ge(y_half, 2 * ch.c + half + 1)
                dve.scalar_tensor_tensor(v, v, ALPHA, bank(6 + half), ALU.mult, ALU.add).then_inc(y_summed, 1)

            def statistics1(ch):
                dve.wait_ge(y_summed, 2 * ch.c + 2)
                for i in range(2):
                    last = dve.bn_stats(st_c[:, i, :], xin[ch.b][:, i * 512:(i + 1) * 512])
                wait_apart(dve, dve_own, own.done(last))
                dve.bn_aggr(mv_c, st_c).then_inc(r_stats, 1)

            def norm1(ch):
                v = xin[ch.b]
                dve.wait_ge(r_std, ch.c + 1)
                own.link(dve.reciprocal(rs_c, rs_c))
                own.link(dve.tensor_scalar(v, v, mv_c[:, 0:1], rs_c, ALU.subtract, ALU.mult))

            def scale1(ch):
                v = xin[ch.b]
                dve.wait_ge(ln1_in, 48)
                own.link(dve.tensor_tensor(v, v, ln1[:, 0, :], ALU.mult))
                dve.wait_ge(x1_out, PRIMED + 16 * ch.c)
                dve.wait_ge(x1T_ps, PRIMED + ch.c)
                dve.tensor_tensor(x1s, v, ln1[:, 1, :], ALU.add).then_inc(x1_ready, 1)

            def sum_numerators(ch):
                dve.wait_ge(inter_sb, ch.c + 1)
                for i in range(2):
                    v = num[:, 2 * i:2 * i + 2, :]
                    last = dve.tensor_tensor(v, psum[:, 2 + i, 0:2 * (DH + 1)].rearrange("p (h n) -> p h n", h=2), v, ALU.add)
                last.then_inc(num_sb, 1)

            def update_state(ch):
                dve.wait_ge(state_ps, ch.c + 1)
                for h in range(HEADS):
                    o = (h % 2) * (DH + 1)
                    last = dve.scalar_tensor_tensor(C[:, h, :], C[:, h, :], w4[:, 1, bass.ds(ch.c * HEADS + h, 1)],
                                                    psum[:, 4 + h // 2, o:o + DH + 1], ALU.mult, ALU.add)
                last.then_inc(c_sb, 1)

            def divide(ch):
                dve.wait_ge(num_sb, ch.c + 1)
                d = num[:, :, DH:DH + 1]
                own.link(dve.scalar_tensor_tensor(den.unsqueeze(2), d, -1.0, d, ALU.mult, ALU.max))
                own.link(dve.tensor_tensor(den, den, w4[:, 3, bass.ds(ch.c * HEADS, HEADS)], ALU.max))
                own.link(dve.reciprocal(den, den))
                if ch.n:
                    dve.wait_ge(hT_ps, ch.c)
                own.link(dve.tensor_tensor(ha, num[:, :, 0:DH], den.unsqueeze(2).to_broadcast([P, HEADS, DH]), ALU.mult))
                for h in range(HEADS):
                    last = dve.bn_stats(st_b[:, h, :], ha[:, h, :])
                wait_apart(dve, dve_own, own.done(last))
                for h in range(HEADS):
                    last = dve.bn_aggr(mv_b[:, h, :], st_b[:, h, :])
                last.then_inc(h_stats, 1)

            def finish_h(ch):
                dve.wait_ge(h_std, ch.c + 1)
                own.link(dve.reciprocal(rs_b, rs_b))
                for h in range(HEADS):
                    last = dve.tensor_scalar(ha[:, h, :], ha[:, h, :], mv_b[:, h, 0:1], rs_b[:, h:h + 1], ALU.subtract, ALU.mult)
                own.link(last)
                dve.wait_ge(og_hb_in[ch.b], 32 * ch.r + 32)
                dve.tensor_tensor(ha, ha, og[ch.b], ALU.mult).then_inc(ha_ready, 1)

            def read_logits(ch):
                dve.wait_ge(lg_ps, PRIMED + ch.c + 1)
                dve.tensor_copy(logits[:, bass.ds(ch.c, 1), :], bank(2)[:, 0:NE].unsqueeze(1)).then_inc(lg_read, 1)

            def split_h(ch):
                xr = XRb[ch.b]
                dve.wait_ge(xr_hi, ch.c + 1)
                for v, src in ((slice(0, 4), bank(0).rearrange("p (h n) -> p h n", h=HEADS)),
                               (slice(4, 6), bank(1)[:, 0:256].rearrange("p (h n) -> p h n", h=2)),
                               (slice(6, 8), acc[:, :, bass.ds(ch.c * P, P)])):
                    last = dve.tensor_tensor(xr[:, 1, v, :], src, xr[:, 0, v, :].bitcast(F32), ALU.subtract)
                last.then_inc(xr_lo, 1)

            def step(ch):
                n = ch.n
                mixes, projects, norms = n < T, 1 <= n <= T, n >= 2
                if norms:
                    residual1(ch.plus(-2), 1)
                    statistics1(ch.plus(-2))
                    norm1(ch.plus(-2))
                if mixes:
                    sum_numerators(ch)
                    divide(ch)
                if n == 0:
                    split_wout(range(4, 6))
                if norms:
                    scale1(ch.plus(-2))
                if mixes:
                    finish_h(ch)
                    update_state(ch)
                if n < T - 1:
                    weigh_scores(ch.plus(1))
                if projects:
                    residual1(ch.plus(-1), 0)
                if n == 0:
                    dve.wait_ge(cv_done, 1)
                if mixes:
                    split_h(ch)
                if n == 0:
                    split_wout(range(6, KC))
                if norms:
                    read_logits(ch.plus(-2))

            weigh_scores(Chunk(0, 0, 0))
            split_wout(range(4))
            dve.wait_ge(c_sb, 1)
            chunk_steps(dve, step, own)
            dve_experts(dve, own)


_INS = ["x", "w_in", "b_in", "mlstm_norm_w", "gmlp_norm_w", "gmlp_norm_b", "gmlp_ws", "gmlp_bs", "conv_w", "conv_b",
        "conv_norm_w", "conv_norm_b", "w_out", "ln1_w", "ln1_b", "router_w", "router_b", "w_gate", "w_up", "w_down",
        "ln2_w", "ln2_b"]


def kernel(**inputs):
    import concourse.bacc as bacc
    from concourse.bass_utils import run_bass_kernel_spmd

    nc = bacc.Bacc("TRN2", target_bir_lowering=False, num_devices=1)
    arrays, args = {}, []
    for name in _INS:
        a = np.ascontiguousarray(inputs[name])
        arrays[f"in_{name}"] = a
        args.append(nc.dram_tensor(f"in_{name}", a.shape, mybir.dt.from_np(a.dtype), kind="ExternalInput").ap())
    args.append(nc.dram_tensor("out_dram", (1, SEQ, D), F32, kind="ExternalOutput").ap())
    hybrid_kernel(nc, *args)
    r = run_bass_kernel_spmd(nc, [arrays], core_ids=[0])
    return r.results[0]["out_dram"]
```
